# Optimizing a Trainium2 kernel written in Bass

```python
import math
import jax, jax.numpy as jnp
from jax import lax
import numpy as np

D_MODEL = 1024
BATCH = 1
SEQ = 128
DEPTH = 2
DEC_BATCH = 1
DEC_SEQ = 512
PAST_LEN = 128

GRID_W = 64
HEAD_DIM = 64
AXIS_DIM = HEAD_DIM // 2
GQA_HEADS = 8
GQA_KV_HEADS = 2
DIFF_HEADS = 4
FOURIER_GROUPS = 4
FOURIER_GROUP_DIM = 128
FOURIER_WIDTH = FOURIER_GROUPS * FOURIER_GROUP_DIM
GQA_WIDTH = GQA_HEADS * HEAD_DIM
GQA_KV_WIDTH = GQA_KV_HEADS * HEAD_DIM
DIFF_QK_WIDTH = DIFF_HEADS * 2 * HEAD_DIM
DIFF_V_WIDTH = DIFF_HEADS * 2 * HEAD_DIM
N_BRANCHES = 3
IN_WIDTH = (FOURIER_WIDTH + GQA_WIDTH + 2 * GQA_KV_WIDTH + 2 * DIFF_QK_WIDTH
            + DIFF_V_WIDTH + N_BRANCHES * D_MODEL)
N_EXPERTS = 16
N_EXPERT_GROUPS = 4
EXPERTS_PER_GROUP = N_EXPERTS // N_EXPERT_GROUPS
TOP_K = 2
D_EXPERT = 256
ROPE_THETA = 10000.0
Q_BLOCK = 128
EPS = 1e-6

kernel_name = 'hybrid_fourier_gqa_diffattn_moe_prefix_dit_step'

F32 = jnp.float32

def _split_points():
    sizes = (FOURIER_WIDTH, GQA_WIDTH, GQA_KV_WIDTH, GQA_KV_WIDTH,
             DIFF_QK_WIDTH, DIFF_QK_WIDTH, DIFF_V_WIDTH, N_BRANCHES * D_MODEL)
    pts, acc = [], 0
    for s in sizes[:-1]:
        acc += s
        pts.append(acc)
    return pts

def rms_norm(x, g):
    xf = x.astype(F32)
    y = xf * lax.rsqrt(jnp.mean(xf * xf, axis=-1, keepdims=True) + EPS)
    return (y * g.astype(F32)).astype(x.dtype)

def adaln(cond, w_mod_l, b_mod_l):
    m = jax.nn.silu(cond) @ w_mod_l + b_mod_l
    return jnp.split(m, 6, axis=-1)

def modulate(h, shift, scale):
    return h * (1 + scale[:, None, :]) + shift[:, None, :]

def axial_rope(n_tokens):
    rows = n_tokens // GRID_W
    row = jnp.repeat(jnp.arange(rows), GRID_W).astype(F32)
    col = jnp.tile(jnp.arange(GRID_W), rows).astype(F32)
    inv = ROPE_THETA ** (-(jnp.arange(AXIS_DIM // 2, dtype=F32) * 2.0 / AXIS_DIM))
    ang_r = row[:, None] * inv[None, :]
    ang_c = col[:, None] * inv[None, :]
    ang = jnp.concatenate([ang_r, ang_r, ang_c, ang_c], axis=-1)
    return jnp.cos(ang), jnp.sin(ang)

def _rotate_half_axial(x):
    x1, x2, x3, x4 = jnp.split(x, 4, axis=-1)
    return jnp.concatenate([-x2, x1, -x4, x3], axis=-1)

def apply_rope(x, cos, sin):
    shp = (1, x.shape[1]) + (1,) * (x.ndim - 3) + (HEAD_DIM,)
    xf = x.astype(F32)
    return (xf * cos.reshape(shp) + _rotate_half_axial(xf) * sin.reshape(shp)).astype(x.dtype)

def mixer_projections(h, w_in_l, q_norm_l, k_norm_l):
    B, N, _ = h.shape
    z = jnp.einsum('bnd,de->bne', h, w_in_l)
    u_f, q_g, k_g, v_g, q_d, k_d, v_d, gates = jnp.split(z, _split_points(), axis=-1)
    q_g = rms_norm(q_g.reshape(B, N, GQA_HEADS, HEAD_DIM), q_norm_l)
    k_g = rms_norm(k_g.reshape(B, N, GQA_KV_HEADS, HEAD_DIM), k_norm_l)
    v_g = v_g.reshape(B, N, GQA_KV_HEADS, HEAD_DIM)
    q_d = q_d.reshape(B, N, DIFF_HEADS, 2, HEAD_DIM)
    k_d = k_d.reshape(B, N, DIFF_HEADS, 2, HEAD_DIM)
    v_d = v_d.reshape(B, N, DIFF_HEADS, 2 * HEAD_DIM)
    return u_f, q_g, k_g, v_g, q_d, k_d, v_d, gates

def fourier_mix(u):
    B, N, _ = u.shape
    ug = u.astype(F32).reshape(B, N, FOURIER_GROUPS, FOURIER_GROUP_DIM)
    y = jnp.real(jnp.fft.fftn(ug, axes=(1, 3), norm='ortho'))
    return y.reshape(B, N, FOURIER_WIDTH).astype(u.dtype)

def gqa_attention(q, k, v):
    B, Nq, H, d = q.shape
    G = H // GQA_KV_HEADS
    nblk = Nq // Q_BLOCK
    qb = q.reshape(B, nblk, Q_BLOCK, GQA_KV_HEADS, G, d).transpose(1, 0, 2, 3, 4, 5)
    scale = d ** -0.5

    def one_block(qi):
        s = jnp.einsum('bqhgd,bkhd->bhgqk', qi, k, preferred_element_type=F32) * scale
        p = jax.nn.softmax(s, axis=-1)
        return jnp.einsum('bhgqk,bkhd->bqhgd', p.astype(v.dtype), v)

    o = lax.map(one_block, qb)
    return o.transpose(1, 0, 2, 3, 4, 5).reshape(B, Nq, H * d)

def diff_attention(q, k, v, lam_params, lambda_init, subln_g):
    B, Nq, H, _, d = q.shape
    lp = lam_params.astype(F32)
    lam = jnp.exp(jnp.sum(lp[0] * lp[1])) - jnp.exp(jnp.sum(lp[2] * lp[3])) + lambda_init
    nblk = Nq // Q_BLOCK
    qb = q.reshape(B, nblk, Q_BLOCK, H, 2, d).transpose(1, 0, 2, 3, 4, 5)
    scale = d ** -0.5

    def one_block(qi):
        s = jnp.einsum('bqhmd,bkhmd->bhmqk', qi, k, preferred_element_type=F32) * scale
        p = jax.nn.softmax(s, axis=-1)
        a = p[:, :, 0] - lam * p[:, :, 1]
        return jnp.einsum('bhqk,bkhe->bqhe', a.astype(v.dtype), v)

    o = lax.map(one_block, qb)
    o = o.transpose(1, 0, 2, 3, 4).reshape(B, Nq, H, 2 * d)
    o = rms_norm(o, subln_g) * (1.0 - lambda_init)
    return o.reshape(B, Nq, DIFF_V_WIDTH)

def merge_branches(u_f, o_g, o_d, gates, w_f, w_go, w_do, w_out):
    g_f, g_g, g_d = jnp.split(jax.nn.sigmoid(gates), N_BRANCHES, axis=-1)
    merged = (g_f * (fourier_mix(u_f) @ w_f)
              + g_g * (o_g @ w_go)
              + g_d * (o_d @ w_do))
    return merged @ w_out

def moe(h, w_router, router_bias, w_gate_l, w_up_l, w_down_l):
    B, N, D = h.shape
    t = h.reshape(B * N, D)
    scores = jax.nn.sigmoid((t @ w_router).astype(F32))
    sel = scores + router_bias.astype(F32)
    grp = sel.reshape(-1, N_EXPERT_GROUPS, EXPERTS_PER_GROUP)
    grp_score = lax.top_k(grp, TOP_K)[0].sum(-1)
    best = jnp.argmax(grp_score, axis=-1)
    in_best = jax.nn.one_hot(best, N_EXPERT_GROUPS, dtype=F32)[:, :, None] > 0
    masked = jnp.where(in_best, grp, -jnp.inf).reshape(-1, N_EXPERTS)
    _, idx = lax.top_k(masked, TOP_K)
    w = jnp.take_along_axis(scores, idx, axis=-1)
    w = w / jnp.sum(w, axis=-1, keepdims=True)
    combine = jnp.sum(jax.nn.one_hot(idx, N_EXPERTS, dtype=F32) * w[..., None], axis=1)
    gate = jnp.einsum('td,edf->tef', t, w_gate_l)
    up = jnp.einsum('td,edf->tef', t, w_up_l)
    act = jax.nn.silu(gate) * up * combine[..., None].astype(gate.dtype)
    return jnp.einsum('tef,efd->td', act, w_down_l).reshape(B, N, D)

def setup_inputs(seed: int = 0) -> dict:
    key = jax.random.key(seed)
    ks = jax.random.split(key, 32)
    D = D_MODEL

    def nrm(k, shape, scale):
        return jax.random.normal(k, shape, F32) * scale

    def gain(k, shape):
        return 1.0 + 0.02 * jax.random.normal(k, shape, F32)

    return {
        'x_prompt': nrm(ks[0], (BATCH, SEQ, D), 1.0),
        'x_sample': nrm(ks[1], (DEC_BATCH, DEC_SEQ, D), 1.0),
        'cache_gqa_k': nrm(ks[2], (DEC_BATCH, DEPTH, PAST_LEN, GQA_KV_HEADS, HEAD_DIM), 1.0),
        'cache_gqa_v': nrm(ks[3], (DEC_BATCH, DEPTH, PAST_LEN, GQA_KV_HEADS, HEAD_DIM), 1.0),
        'cache_diff_k': nrm(ks[4], (DEC_BATCH, DEPTH, PAST_LEN, DIFF_HEADS, 2, HEAD_DIM), 1.0),
        'cache_diff_v': nrm(ks[5], (DEC_BATCH, DEPTH, PAST_LEN, DIFF_HEADS, 2 * HEAD_DIM), 1.0),
        'c': nrm(ks[6], (DEC_BATCH, D), 1.0),
        'c_ctx': nrm(ks[7], (D,), 1.0),
        'norm1_g': gain(ks[8], (DEPTH, D)),
        'w_mod': nrm(ks[9], (DEPTH, D, 6 * D), 0.5 * D ** -0.5),
        'b_mod': nrm(ks[10], (DEPTH, 6 * D), 0.01),
        'w_in': nrm(ks[11], (DEPTH, D, IN_WIDTH), D ** -0.5),
        'gqa_q_norm': gain(ks[12], (DEPTH, HEAD_DIM)),
        'gqa_k_norm': gain(ks[13], (DEPTH, HEAD_DIM)),
        'diff_lambda': nrm(ks[14], (DEPTH, 4, HEAD_DIM), 0.1),
        'diff_subln_g': gain(ks[15], (DEPTH, 2 * HEAD_DIM)),
        'w_fourier': nrm(ks[16], (DEPTH, FOURIER_WIDTH, D), FOURIER_WIDTH ** -0.5),
        'w_gqa_o': nrm(ks[17], (DEPTH, GQA_WIDTH, D), GQA_WIDTH ** -0.5),
        'w_diff_o': nrm(ks[18], (DEPTH, DIFF_V_WIDTH, D), DIFF_V_WIDTH ** -0.5),
        'w_out': nrm(ks[19], (DEPTH, D, D), D ** -0.5),
        'norm2_g': gain(ks[20], (DEPTH, D)),
        'w_router': nrm(ks[21], (D, N_EXPERTS), D ** -0.5),
        'router_bias': nrm(ks[22], (N_EXPERTS,), 0.01),
        'w_e_gate': nrm(ks[23], (DEPTH, N_EXPERTS, D, D_EXPERT), D ** -0.5),
        'w_e_up': nrm(ks[24], (DEPTH, N_EXPERTS, D, D_EXPERT), D ** -0.5),
        'w_e_down': nrm(ks[25], (DEPTH, N_EXPERTS, D_EXPERT, D), D_EXPERT ** -0.5),
        'final_norm_g': gain(ks[26], (D,)),
    }

def reference(x_prompt, x_sample, cache_gqa_k, cache_gqa_v, cache_diff_k, cache_diff_v,
              c, c_ctx, norm1_g, w_mod, b_mod, w_in, gqa_q_norm, gqa_k_norm,
              diff_lambda, diff_subln_g, w_fourier, w_gqa_o, w_diff_o, w_out, norm2_g,
              w_router, router_bias, w_e_gate, w_e_up, w_e_down, final_norm_g):
    xp = x_prompt
    ks_g, vs_g, ks_d, vs_d = [], [], [], []
    for l in range(DEPTH):
        lambda_init = 0.8 - 0.6 * math.exp(-0.3 * l)
        sh1, sc1, g1, sh2, sc2, g2 = adaln(c_ctx[None, :], w_mod[l], b_mod[l])
        h = modulate(rms_norm(xp, norm1_g[l]), sh1, sc1)
        u_f, q_g, k_g, v_g, q_d, k_d, v_d, gates = mixer_projections(
            h, w_in[l], gqa_q_norm[l], gqa_k_norm[l])
        o_g = gqa_attention(q_g, k_g, v_g)
        o_d = diff_attention(q_d, k_d, v_d, diff_lambda[l], lambda_init, diff_subln_g[l])
        xp = xp + g1[:, None, :] * merge_branches(u_f, o_g, o_d, gates, w_fourier[l],
                                                  w_gqa_o[l], w_diff_o[l], w_out[l])
        h = modulate(rms_norm(xp, norm2_g[l]), sh2, sc2)
        xp = xp + g2[:, None, :] * moe(h, w_router, router_bias, w_e_gate[l], w_e_up[l], w_e_down[l])
        ks_g.append(k_g)
        vs_g.append(v_g)
        ks_d.append(k_d)
        vs_d.append(v_d)
    y_prompt = rms_norm(xp, final_norm_g)
    new_gqa_k = jnp.stack(ks_g, axis=1)
    new_gqa_v = jnp.stack(vs_g, axis=1)
    new_diff_k = jnp.stack(ks_d, axis=1)
    new_diff_v = jnp.stack(vs_d, axis=1)

    cos, sin = axial_rope(x_sample.shape[1])
    xs = x_sample
    for l in range(DEPTH):
        lambda_init = 0.8 - 0.6 * math.exp(-0.3 * l)
        sh1, sc1, g1, sh2, sc2, g2 = adaln(c, w_mod[l], b_mod[l])
        h = modulate(rms_norm(xs, norm1_g[l]), sh1, sc1)
        u_f, q_g, k_g, v_g, q_d, k_d, v_d, gates = mixer_projections(
            h, w_in[l], gqa_q_norm[l], gqa_k_norm[l])
        q_g = apply_rope(q_g, cos, sin)
        k_g = apply_rope(k_g, cos, sin)
        q_d = apply_rope(q_d, cos, sin)
        k_d = apply_rope(k_d, cos, sin)
        k_g = jnp.concatenate([cache_gqa_k[:, l].astype(k_g.dtype), k_g], axis=1)
        v_g = jnp.concatenate([cache_gqa_v[:, l].astype(v_g.dtype), v_g], axis=1)
        k_d = jnp.concatenate([cache_diff_k[:, l].astype(k_d.dtype), k_d], axis=1)
        v_d = jnp.concatenate([cache_diff_v[:, l].astype(v_d.dtype), v_d], axis=1)
        o_g = gqa_attention(q_g, k_g, v_g)
        o_d = diff_attention(q_d, k_d, v_d, diff_lambda[l], lambda_init, diff_subln_g[l])
        xs = xs + g1[:, None, :] * merge_branches(u_f, o_g, o_d, gates, w_fourier[l],
                                                  w_gqa_o[l], w_diff_o[l], w_out[l])
        h = modulate(rms_norm(xs, norm2_g[l]), sh2, sc2)
        xs = xs + g2[:, None, :] * moe(h, w_router, router_bias, w_e_gate[l], w_e_up[l], w_e_down[l])
    y_sample = rms_norm(xs, final_norm_g)

    return (y_prompt, y_sample, new_gqa_k, new_gqa_v, new_diff_k, new_diff_v)


_drawn_inputs = setup_inputs


def setup_inputs(seed=0):
    import zlib

    import numpy as np

    out = dict(_drawn_inputs(seed))
    spreads = {}
    factors = {'cache_gqa_k': 3.286,
     'norm1_g': 2.932,
     'gqa_q_norm': 8.0,
     'gqa_k_norm': 2.76,
     'diff_subln_g': 4.483,
     'final_norm_g': 7.798,
     'cache_diff_k': 8.0,
     'cache_diff_v': 8.0}
    for name, (base, spread) in spreads.items():
        noise = np.random.default_rng([zlib.crc32(name.encode()), seed]).standard_normal(out[name].shape)
        drawn = base * np.exp(spread * noise) if base else spread * noise
        out[name] = __import__('jax').numpy.asarray(drawn.astype(out[name].dtype))
    for name, factor in factors.items():
        out[name] = (out[name] * factor).astype(out[name].dtype)
    return out
```

```python
from contextlib import ExitStack

import numpy as np
import concourse.bass as bass
from concourse import mybir

F32 = mybir.dt.float32
F32R = mybir.dt.float32r
ALU = mybir.AluOpType
ACT = mybir.ActivationFunctionType
AX = mybir.AxisListType

P = 128
D = 1024
KD = D // P
DEPTH = 2
N_PROMPT, N_SAMPLE, N_PAST = 128, 512, 128
TOK = N_PROMPT + N_SAMPLE
TT = TOK // P
HALF = TOK // 2
KEYS = N_PAST + N_SAMPLE
HD = 64
QH, KVH, DH = 8, 2, 4
FG, FGD = 4, 128
BW = 512
IN_COLS = 2816
WC = 256
NE, NG, EPG = 16, 4, 4
DE = 256
EPS = 1e-6
CH_QG, CH_KVG, CH_QD, CH_KD, CH_VD, CH_GATE = 2, 4, 5, 7, 9, 11
N_WIN = CH_GATE
N_STREAM = N_WIN + 12 + 4
SCALE = HD ** -0.5


def build(nc, a, debug=None):
    names = set()

    with ExitStack() as ctx:
        ctx.enter_context(nc.allow_non_contiguous_dma(reason="small strided loads"))
        base = (nc.sbuf_base + 63) // 64 * 64

        def at(name, shape, off, dt=F32):
            assert name not in names and off % 32 == 0
            names.add(name)
            return nc.alloc_sbuf_tensor_at(name, shape, dt, offset=base + off)

        K = 1024
        x_T = at("x_T", [P, KD, TOK], 0)
        h_hi = at("h_hi", [P, KD, TOK], 20 * K, F32R)
        h_lo = at("h_lo", [P, KD, TOK], 40 * K, F32R)
        o = 60 * K
        ident = at("ident", [P, P], o)
        ones = at("ones", [P, P], o + 512)
        cond_T = at("cond_T", [P, KD, 2], o + 1024)
        mod_T = at("mod_T", [P, 48, 2], o + 1088)
        gain_T = at("gain_T", [P, 16], o + 1472)
        mul1 = at("mul1", [P, KD, 2], o + 1536)
        mul2 = at("mul2", [P, KD, 2], o + 1600)
        fin_gain = at("fin_gain", [P, KD], o + 1664)
        qk_gain = at("qk_gain", [P, 2, HD], o + 1696)
        sub_gain = at("sub_gain", [P, 1], o + 2208)
        lam_c = at("lam_c", [P, 2], o + 2240)
        neg_lam = at("neg_lam", [P, 1], o + 2272)
        wr_hi = at("wr_hi", [P, KD, NE], o + 2304, F32R)
        wr_lo = at("wr_lo", [P, KD, NE], o + 2816, F32R)
        bias_bc = at("bias_bc", [P, NE], o + 3328)
        tie = at("tie", [P, 4, 4], o + 3392)
        small = at("small_stats", [P, 4, 8], o + 3456)
        od_ss = at("od_ss", [P, TT * DH], o + 3584)
        od_r = at("od_r", [P, TT * DH], o + 3680)
        Z = o + 3776
        Z = (Z + 63) // 64 * 64
        LIMIT = nc.sbuf_usable_end - base

        psum = ctx.enter_context(nc.psum_tensor("psum", [P, 8, 512], F32))

        def pair(n):
            return psum[:, 2 * (n % 4):2 * (n % 4) + 2, :]

        def flat(n):
            return pair(n).rearrange("p a b -> p (a b)")

        sems = []

        def sem(name):
            s = ctx.enter_context(nc.semaphore(name))
            sems.append(s)
            return s

        comb_dram = nc.dram_tensor("comb_dram", (NE, TOK), F32, kind="Internal").ap()

        s_small = sem("small_loaded")
        s_store = sem("stores_done")
        n_sq, n_sum, n_var, n_std, n_rstd = (sem(x) for x in
                                             ("norm_squares", "norm_summed", "norm_var", "norm_std", "norm_rstd"))
        n_t, n_h, n_hi, n_lo = (sem(x) for x in ("norm_scaled", "norm_h", "norm_hi", "norm_lo"))

        def clear():
            ids = [s.num for s in sems]
            nc.all_engine_barrier(sems_to_clear=range(min(ids), max(ids) + 1))

        def norm_bufs(tag, off):
            return dict(sq=at(f"sq_{tag}", [P, 2, TOK], off), var=at(f"var_{tag}", [P, TOK], off + 5 * K),
                        rstd=at(f"rstd_{tag}", [P, TOK], off + 7680), h=at(f"h_{tag}", [P, 2, TOK], off + 10 * K))

        def norm_pe(pe, nb):
            for kc in range(KD):
                pe.wait_ge(n_sq, kc + 1)
                for hf in range(2):
                    mm = pe.matmul(pair(3)[:, hf, 0:HALF], ones[:, :], nb["sq"][:, kc % 2, hf * HALF:(hf + 1) * HALF],
                                   start=(kc == 0), stop=(kc == KD - 1))
                mm.then_inc(n_sum, 1)

        def norm_act_squares(act, nb):
            for kc in range(KD):
                if kc >= 2:
                    act.wait_ge(n_sum, kc - 1)
                act.activation(nb["sq"][:, kc % 2, :], x_T[:, kc, :], ACT.Square).then_inc(n_sq, 1)
            act.wait_ge(n_var, 1)
            act.activation(nb["var"][:, :], nb["var"][:, :], ACT.Sqrt).then_inc(n_std, 1)

        def norm_act_modulate(act, nb, mul, shift):
            for kc in range(KD):
                act.wait_ge(n_t, kc + 1)
                for s, (c0, c1) in enumerate(((0, N_PROMPT), (N_PROMPT, TOK))):
                    act.activation(nb["h"][:, kc % 2, c0:c1], nb["h"][:, kc % 2, c0:c1], ACT.Identity,
                                   bias=shift[:, kc, s:s + 1], scale=mul[:, kc, s:s + 1]).then_inc(n_h, 1)
                act.wait_ge(n_h, 2 * kc + 2)
                act.activation(h_hi[:, kc, :], nb["h"][:, kc % 2, :], ACT.Copy).then_inc(n_hi, 1)

        def norm_dve(dve, nb, free):
            dve.wait_ge(n_sum, KD)
            dve.tensor_scalar(nb["var"][:, :].rearrange("p (a b) -> p a b", a=2), pair(3)[:, :, 0:HALF],
                              1.0 / D, EPS, ALU.mult, ALU.add).then_inc(n_var, 1)
            dve.wait_ge(n_std, 1)
            dve.reciprocal(nb["rstd"][:, :], nb["var"][:, :]).then_inc(n_rstd, 1)
            dve.wait_ge(n_rstd, 1)
            for kc in range(KD):
                if kc >= 2:
                    dve.wait_ge(free, kc - 1)
                dve.tensor_tensor(nb["h"][:, kc % 2, :], x_T[:, kc, :], nb["rstd"][:, :], ALU.mult).then_inc(n_t, 1)

        def norm_pool(pool, nb):
            for kc in range(KD):
                pool.wait_ge(n_hi, kc + 1)
                pool.tensor_tensor(h_lo[:, kc, :], nb["h"][:, kc % 2, :], h_hi[:, kc, :].bitcast(F32),
                                   ALU.subtract).then_inc(n_lo, 1)

        def mm_split(pe, out, st_hi, st_lo, mv_hi, mv_lo, start, stop):
            for n, (st, mv) in enumerate(((st_hi, mv_hi), (st_hi, mv_lo), (st_lo, mv_hi))):
                for q, dst in enumerate(out):
                    mm = pe.matmul(dst, st, mv[q], start=start and n == 0, stop=stop and n == 2)
            return mm

        def add_gated(dve, f, src, gate, done):
            parts = ((0, 0, 0, P), (1, 0, P, HALF), (1, 1, 0, HALF))
            for s, hf, c0, c1 in parts:
                xs = x_T[:, f, hf * HALF + c0:hf * HALF + c1]
                ins = dve.scalar_tensor_tensor(out=xs, in0=src[:, hf, c0:c1], scalar=gate[:, f, s:s + 1], in1=xs,
                                               op0=ALU.mult, op1=ALU.add)
            ins.then_inc(done, 1)

        s_xl, s_xt, s_xe, s_c1, s_c2, s_c3, s_c4, s_w1, s_w2 = (sem(x) for x in (
            "x_loaded", "x_turned", "x_evacuated", "cond_sigmoid", "cond_silu", "cond_turned", "cond_kept",
            "router_hi", "router_lo"))
        x_tok = at("x_tok", [P, TT, D], Z)
        cond_r = at("cond_r", [2, D], Z + 20 * K)
        cond_s = at("cond_s", [2, D], Z + 24 * K)
        cond_u = at("cond_u", [2, D], Z + 28 * K)
        wr_raw = at("wr_raw", [P, KD, NE], Z + 32 * K)
        fg_raw = at("fg_raw", [KD, P], Z + 33 * K)
        N_SMALL0 = 9
        with nc.Block() as block:
            @block.sync
            def _(sp):
                sp.dma_start(ident[:, :], a["c_ident"]).then_inc(s_small, 16)
                sp.dma_start(ones[:, :], a["c_ones"]).then_inc(s_small, 16)
                sp.dma_start(x_tok[:, 0, :], a["x_prompt"][0]).then_inc(s_xl, 16)
                sp.dma_start(x_tok[:, 1:TT, :], a["x_sample"][0].rearrange("(t p) d -> p t d", p=P)).then_inc(s_xl, 16)
                sp.dma_start(cond_r[0:1, :], a["c_ctx"].rearrange("(a n) -> a n", a=1)).then_inc(s_small, 16)
                sp.dma_start(cond_r[1:2, :], a["c"]).then_inc(s_small, 16)
                sp.dma_start(wr_raw[:, :, :], a["w_router"].rearrange("(k p) e -> p k e", p=P)).then_inc(s_small, 16)
                sp.dma_start(fg_raw[:, :], a["final_norm_g"].rearrange("(k p) -> k p", p=P)).then_inc(s_small, 16)
                sp.dma_start(bias_bc[:, :], a["router_bias"].partition_broadcast(P)).then_inc(s_small, 16)
                sp.dma_start(tie[:, :, :], a["c_tie"].partition_broadcast(P)).then_inc(s_small, 16)
                sp.dma_start(lam_c[:, :], a["c_lambda"][0].partition_broadcast(P)).then_inc(s_small, 16)
                sp.wait_ge(s_small, 16 * N_SMALL0)

            @block.tensor
            def _(pe):
                pe.wait_ge(s_small, 16 * N_SMALL0)
                pe.wait_ge(s_xl, 32)
                for kc in range(KD):
                    if kc >= 3:
                        pe.wait_ge(s_xe, kc - 2)
                    for t in range(TT):
                        mm = pe.transpose(flat(kc % 3)[:, t * P:(t + 1) * P], x_tok[:, t, kc * P:(kc + 1) * P],
                                          ident[:, :])
                    mm.then_inc(s_xt, 1)
                pe.wait_ge(s_c2, 1)
                for kc in range(KD):
                    pe.transpose(flat(3)[:, 2 * kc:2 * kc + 2], cond_u[:, kc * P:(kc + 1) * P], ident[0:2, 0:2])
                pe.transpose(flat(3)[:, 512:512 + KD], fg_raw[:, :], ident[0:KD, 0:KD]).then_inc(s_c3, 1)

            @block.scalar
            def _(act):
                act.wait_ge(s_small, 16 * N_SMALL0)
                act.activation(cond_s[:, :], cond_r[:, :], ACT.Sigmoid).then_inc(s_c1, 1)
                act.activation(wr_hi[:, :, :], wr_raw[:, :, :], ACT.Copy).then_inc(s_w1, 1)

            @block.vector
            def _(dve):
                dve.wait_ge(s_c1, 1)
                dve.tensor_tensor(cond_u[:, :], cond_r[:, :], cond_s[:, :], ALU.mult).then_inc(s_c2, 1)
                dve.wait_ge(s_w1, 1)
                dve.tensor_tensor(wr_lo[:, :, :], wr_raw[:, :, :], wr_hi[:, :, :].bitcast(F32),
                                  ALU.subtract).then_inc(s_w2, 1)
                for kc in range(KD):
                    dve.wait_ge(s_xt, kc + 1)
                    dve.tensor_copy(x_T[:, kc, :], flat(kc % 3)[:, 0:TOK]).then_inc(s_xe, 1)
                dve.wait_ge(s_c3, 1)
                dve.tensor_copy(cond_T[:, :, :], flat(3)[:, 0:2 * KD].rearrange("p (k s) -> p k s", s=2)).then_inc(s_c4, 1)
                dve.tensor_copy(fin_gain[:, :], flat(3)[:, 512:512 + KD]).then_inc(s_c4, 1)
        clear()

        MC = 6 * D // 512
        wm = [at(f"wm{i}", [P, KD, 512], Z + 16 * K * i) for i in range(3)]
        mod_rows = at("mod_rows", [2, 6 * D], Z + 48 * K)
        mod_bias = at("mod_bias", [1, 6 * D], Z + 72 * K)
        gain_rows = at("gain_rows", [16, P], Z + 96 * K)
        lam_in = at("lam_in", [P, 2, 2, HD], Z + 97 * K)
        lam_pr = at("lam_pr", [P, 2, HD], Z + 98 * K)
        lam_s = at("lam_s", [P, 2], Z + 99 * K)
        lam_e = at("lam_e", [P, 2], Z + 99 * K + 32)
        lam_d = at("lam_d", [P, 1], Z + 99 * K + 64)
        sub_raw = at("sub_raw", [P, 1], Z + 99 * K + 96)
        m_ld = [sem(f"wmod_loaded{i}") for i in range(3)]
        m_mm, m_ev, m_tr, m_cp, m_l = (sem(x) for x in
                                       ("mod_product", "mod_evacuated", "mod_turned", "mod_kept", "lambda_step"))

        M = Z
        raw = [at(f"raw{i}", [P, KD, WC], M + 8 * K * i) for i in range(2)]
        whi = [at(f"whi{i}", [P, KD, WC], M + 16 * K + 8 * K * i, F32R) for i in range(2)]
        wlo = [at(f"wlo{i}", [P, KD, WC], M + 32 * K + 8 * K * i, F32R) for i in range(2)]
        M += 48 * K
        pw = [at(f"pw{i}", [P, 4, WC], M + 4 * K * i) for i in range(2)]
        M += 8 * K
        y_T = at("y_T", [P, FG, TOK], M)
        q_T = at("q_T", [P, 8, TOK], M + 10 * K)
        k_T = at("k_T", [P, 6, KEYS + N_PROMPT], M + 30 * K)
        v_tok = at("v_tok", [P, 6, 640], M + 48 * K)
        R = M + 63 * K
        assert R + 25 * K <= LIMIT, (R + 25 * K, LIMIT)
        u_T = at("u_T", [P, FG, TOK], M + 10 * K)
        dft_tab = at("dft_tab", [P, 2, 4, 512], M + 20 * K)
        dft_ch = at("dft_ch", [P, 2 * P], M + 36 * K)
        dft_pr = at("dft_pr", [P, 2, P], M + 37 * K)
        ab = at("ab", [P, 2, TT, 2 * P], M + 38 * K)
        nb_mix = norm_bufs("mix", R)
        z_s = at("z_s", [P, 4, WC], R)
        z_r = at("z_r", [P, 4, WC], R + 4 * K)
        z_t = at("z_t", [P, WC], R + 8 * K)
        z_q = at("z_q", [P, WC], R + 9 * K)
        z_ss = at("z_ss", [P, 4], R + 10 * K)
        z_v = at("z_v", [P, 4], R + 10 * K + 32)
        z_d = at("z_d", [P, 4], R + 10 * K + 64)
        z_i = at("z_i", [P, 4], R + 10 * K + 96)
        k_cache = at("k_cache", [P, 6, P], R + 15 * K)
        rope = at("rope", [P, 2, 4, HD], R + 18 * K)
        k_out_g = at("k_out_g", [P, P], R + 20 * K)
        k_out_d = at("k_out_d", [P, 512], R + 20 * K + 512)
        prob = at("prob", [P, 4, KEYS], R)
        prob_T = at("prob_T", [P, 2, 5, P], R + 10 * K)
        od = at("od", [P, TT, DH, P], R + 15 * K)
        mg_hi = at("mg_hi", [P, KD, TOK], M + 30 * K, F32R)
        mg_lo = at("mg_lo", [P, KD, TOK], M + 50 * K, F32R)
        sig_m = at("sig_m", [P, 2, TOK], M + 70 * K)
        mg = at("mg", [P, 2, TOK], M + 75 * K)
        mg_t = at("mg_t", [P, TOK], M + 80 * K)

        w_ld = [sem(f"weights_loaded{i}") for i in range(2)]
        w_hi, w_lo = sem("weights_hi"), sem("weights_lo")
        p_ld = [sem(f"out_weights_loaded{i}") for i in range(2)]
        s_full, s_free = sem("psum_full"), sem("psum_free")
        s_z, s_rope, s_vs, s_va, s_kc, s_cv = (sem(x) for x in (
            "rows_used", "rope_done", "row_square", "row_sqrt", "k_cache_loaded", "v_cache_loaded"))
        s_r = sem("rope_step")
        t_s, t_max, t_exp, t_p, t_tr, t_pt, t_pv, t_o, t_l = (sem(x) for x in (
            "scores_ready", "max_ready", "exp_done", "probs_ready", "probs_turned", "probs_T_kept",
            "pv_ready", "pv_kept", "sum_inverted"))
        d_sq, d_1, d_2, d_3, d_t, d_k = (sem(x) for x in (
            "subln_squares", "subln_var", "subln_sqrt", "subln_scaled", "subln_turned", "subln_kept"))
        g_full, g_sig, g_pfull, g_pfree, g_acc, g_hi, g_lo = (sem(x) for x in (
            "gate_ready", "gate_sigmoid", "branch_ready", "branch_used", "merge_step", "merged_hi", "merged_lo"))
        o_full, o_add = sem("w_out_ready"), sem("residual_added")

        units = [("u", g) for g in range(FG)]
        units += [("ab", 0, 0), ("ab", 0, 1), ("ab", 1, 0), ("ab", 1, 1)]
        for g in range(FG):
            units.append(("y", g))
            if g + 2 < FG:
                units += [("ab", g + 2, 0), ("ab", g + 2, 1)]
        units.append(("kcache",))
        rows = [(c, t) for c in range(CH_QG, N_WIN) for t in range(TT)]
        turned = [r for r in rows if r[0] < CH_VD]
        LAG = 3
        for i in range(len(rows) + LAG):
            if i < len(rows):
                units.append(("z",) + rows[i])
            if LAG <= i < LAG + len(turned):
                units.append(("x",) + turned[i - LAG])
        unit_no = {u: n for n, u in enumerate(units)}
        n_x = {r: n for n, r in enumerate(turned)}

        def is_gqa(c):
            return c < CH_QD

        def key_tile(t):
            return 5 if t == 0 else t

        att = [("g", h, t) for h in range(QH) for t in range(TT)]
        att += [("d", h, t) for h in range(DH) for t in range(TT)]
        maps, first_map = [], []
        for u in att:
            first_map.append(len(maps))
            maps += [u + (m,) for m in range(1 if u[0] == "g" else 2)]
        map_end = first_map[1:] + [len(maps)]

        def q_slice(kind, h, t, m):
            if kind == "g":
                r = HD * (h % 2)
                return q_T[r:r + HD, h // 2, t * P:(t + 1) * P]
            return q_T[HD * m:HD * m + HD, 4 + h, t * P:(t + 1) * P]

        def k_slice(kind, h, m, c0, c1):
            if kind == "g":
                r = HD * (h % 2)
                return k_T[r:r + HD, h // (QH // KVH), c0:c1]
            return k_T[HD * m:HD * m + HD, 2 + h, c0:c1]

        def key_tiles(t):
            return [5] if t == 0 else [0, 1, 2, 3, 4]

        def scores_view(n, t):
            return flat(n % 2)[:, 0:P] if t == 0 else pair(n % 2)[:, :, 0:HALF]

        def prob_view(n, t):
            w = P if t == 0 else KEYS
            v = prob[:, n % 4, 0:w]
            return v if t == 0 else v.rearrange("p (a b) -> p a b", a=2)

        E0 = Z
        ex = {}
        for n, r in enumerate("gud"):
            shape = [P, 2, D] if r == "d" else [P, KD, DE]
            ex[r] = (at(f"xw_raw_{r}", shape, E0 + 24 * K * n), at(f"xw_hi_{r}", shape, E0 + 24 * K * n + 8 * K, F32R),
                     at(f"xw_lo_{r}", shape, E0 + 24 * K * n + 16 * K, F32R))
        E0 += 72 * K
        y_acc = at("y_acc", [P, KD, TOK], E0)
        act_f = at("act_f", [P, 2, TOK], E0 + 20 * K)
        act_hi = at("act_hi", [P, 2, TOK], E0 + 25 * K, F32R)
        act_lo = at("act_lo", [P, 2, TOK], E0 + 30 * K, F32R)
        sig_x = at("sig_x", [P, 2, TOK], E0 + 35 * K)
        cb = at("cb", [P, 2, TOK], E0 + 40 * K)
        nb_moe = norm_bufs("moe", E0 + 45 * K)
        RT = E0 + 60 * K
        comb_T = at("comb_T", [NE, TOK], RT)
        rt_n = [0]

        def rt(name, n):
            rt_n[0] += 1
            return at(name, [P, n], RT + 2560 + 320 * (rt_n[0] - 1))
        sc = rt("rt_scores", TT * NE)
        sel = rt("rt_select", TT * NE)
        rank = rt("rt_rank", TT * NE)
        top2 = rt("rt_top2", TT * NE)
        tmp16 = rt("rt_tmp", TT * NE)
        grp = rt("rt_group", TT * NG)
        grank = rt("rt_grank", TT * NG)
        gbest = rt("rt_gbest", TT * NG)
        wsum = rt("rt_wsum", TT)
        wrec = rt("rt_wrec", TT)
        comb = rt("rt_comb", TT * NE)
        cmp_gt = at("rt_gt", [P, TT * NG * 16], RT + 2560 + 320 * 11)
        cmp_eq = at("rt_eq", [P, TT * NG * 16], RT + 2560 + 320 * 11 + 1280)
        assert RT + 2560 + 320 * 11 + 2560 <= LIMIT
        x_ld = {r: sem(f"expert_{r}_loaded") for r in "gud"}
        x_hi = {r: sem(f"expert_{r}_hi") for r in "gud"}
        x_lo = {r: sem(f"expert_{r}_lo") for r in "gud"}
        r_lg, r_sg, r_st, r_ct, r_ce, r_cs = (sem(x) for x in (
            "router_logits", "router_scores", "routing_step", "combine_turned", "combine_kept", "combine_stored"))
        c_ld = sem("combine_loaded")
        x_full, x_free, x_sig, x_ahi, x_alo, x_sg, x_y0 = (sem(x) for x in (
            "expert_psum_full", "expert_psum_free", "expert_sigmoid", "expert_act_hi",
            "expert_act_lo", "expert_gated", "y_cleared"))
        x_step = sem("moe_residual")
        ROUTE_STEPS = 20

        with nc.Fori(0, DEPTH) as layer:
            with nc.Block() as block:
                @block.sync
                def _(sp):
                    w_mod = a["w_mod"][layer].rearrange("(k p) n -> p k n", p=P)
                    sp.dma_start(mod_bias[:, :], a["b_mod"][layer].rearrange("(a n) -> a n", a=1)).then_inc(s_small, 16)
                    sp.dma_start(gain_rows[0:8, :], a["norm1_g"][layer].rearrange("(k p) -> k p", p=P)).then_inc(s_small, 16)
                    sp.dma_start(gain_rows[8:16, :], a["norm2_g"][layer].rearrange("(k p) -> k p", p=P)).then_inc(s_small, 16)
                    sp.dma_start(qk_gain[:, 0, :], a["gqa_q_norm"][layer].partition_broadcast(P)).then_inc(s_small, 16)
                    sp.dma_start(qk_gain[:, 1, :], a["gqa_k_norm"][layer].partition_broadcast(P)).then_inc(s_small, 16)
                    sp.dma_start(sub_raw[:, :], a["diff_subln_g"][layer].rearrange("(p a) -> p a", a=1)).then_inc(s_small, 16)
                    sp.dma_start(lam_c[:, :], a["c_lambda"][layer].partition_broadcast(P)).then_inc(s_small, 16)
                    sp.dma_start(lam_in[:, :, :, :].rearrange("p a b d -> p (a b) d"),
                                 a["diff_lambda"][layer].partition_broadcast(P)).then_inc(s_small, 16)
                    for j in range(MC):
                        if j >= 3:
                            sp.wait_ge(m_mm, j - 2)
                        sp.dma_start(wm[j % 3][:, :, :], w_mod[:, :, j * 512:(j + 1) * 512]).then_inc(m_ld[j % 3], 16)

                @block.tensor
                def _(pe):
                    pe.wait_ge(s_small, 16 * 8)
                    pe.transpose(psum[:, 6, 0:16], gain_rows[:, :], ident[0:16, 0:16])

                    def turn(j):
                        pe.wait_ge(m_ev, j + 1)
                        for q in range(4):
                            c = 4 * j + q
                            mm = pe.transpose(psum[:, 7, 2 * c:2 * c + 2], mod_rows[:, c * P:(c + 1) * P], ident[0:2, 0:2])
                        mm.then_inc(m_tr, 1)

                    for j in range(MC):
                        pe.wait_ge(m_ld[j % 3], 16 * (j // 3 + 1))
                        if j >= 4:
                            pe.wait_ge(m_ev, j - 3)
                        for kc in range(KD):
                            pe.matmul(psum[0:2, j % 4, :], cond_T[:, kc, :], wm[j % 3][:, kc, :], start=(kc == 0), stop=False)
                        pe.matmul(psum[0:2, j % 4, :], ones[0:1, 0:2], mod_bias[:, j * 512:(j + 1) * 512],
                                  start=False, stop=True).then_inc(m_mm, 1)
                        if j >= 1:
                            turn(j - 1)
                    turn(MC - 1)

                @block.scalar
                def _(act):
                    for j in range(MC):
                        act.wait_ge(m_mm, j + 1)
                        act.activation(mod_rows[:, j * 512:(j + 1) * 512], psum[0:2, j % 4, :], ACT.Copy).then_inc(m_ev, 1)
                    act.wait_ge(m_l, 2)
                    act.activation(lam_e[:, :], lam_s[:, :], ACT.Exp).then_inc(m_l, 1)

                @block.vector
                def _(dve):
                    dve.wait_ge(s_small, 16 * 8)
                    dve.tensor_tensor(lam_pr[:, :, :], lam_in[:, :, 0, :], lam_in[:, :, 1, :], ALU.mult).then_inc(m_l, 1)
                    dve.wait_ge(m_l, 1)
                    dve.tensor_reduce(lam_s[:, :], lam_pr[:, :, :], AX.X, ALU.add).then_inc(m_l, 1)
                    dve.tensor_scalar(sub_gain[:, :], sub_raw[:, :], lam_c[:, 1:2], None, ALU.mult)
                    dve.wait_ge(m_tr, MC)
                    dve.tensor_copy(mod_T[:, :, :], psum[:, 7, 0:96].rearrange("p (c s) -> p c s", s=2)).then_inc(m_cp, 1)
                    dve.tensor_copy(gain_T[:, :], psum[:, 6, 0:16]).then_inc(m_cp, 1)
                    dve.wait_ge(m_cp, 2)
                    for mul, col, g0 in ((mul1, 8, 0), (mul2, 32, 8)):
                        dve.scalar_tensor_tensor(out=mul[:, :, :], in0=mod_T[:, col:col + 8, :], scalar=1.0,
                                                 in1=gain_T[:, g0:g0 + 8].unsqueeze(2).to_broadcast([P, KD, 2]),
                                                 op0=ALU.add, op1=ALU.mult)
                    dve.wait_ge(m_l, 3)
                    dve.tensor_tensor(lam_d[:, :], lam_e[:, 1:2], lam_e[:, 0:1], ALU.subtract).then_inc(m_l, 1)
                    dve.wait_ge(m_l, 4)
                    dve.tensor_tensor(neg_lam[:, :], lam_d[:, :], lam_c[:, 0:1], ALU.subtract).then_inc(m_l, 1)
            clear()

            shift1, gate1 = mod_T[:, 0:8, :], mod_T[:, 16:24, :]
            shift2, gate2 = mod_T[:, 24:32, :], mod_T[:, 40:48, :]
            with nc.Block() as block:
                @block.sync
                def _(sp):
                    w_in = a["w_in"][layer].rearrange("(k p) n -> p k n", p=P)
                    w_out = a["w_out"][layer].rearrange("(k p) n -> p k n", p=P)
                    w_br = [a[n][layer].rearrange("(k p) n -> p k n", p=P) for n in ("w_fourier", "w_gqa_o", "w_diff_o")]

                    def stream(i):
                        if i >= 2:
                            sp.wait_ge(w_lo, i - 1)
                        if i < N_WIN:
                            src = w_in[:, :, i * WC:(i + 1) * WC]
                        elif i < N_WIN + 12:
                            m, b = divmod(i - N_WIN, 3)
                            c0 = IN_COLS + b * D + m * WC
                            src = w_in[:, :, c0:c0 + WC]
                        else:
                            m = i - N_WIN - 12
                            src = w_out[:, :, m * WC:(m + 1) * WC]
                        sp.dma_start(raw[i % 2][:, :, :], src).then_inc(w_ld[i % 2], 16)

                    stream(0)
                    stream(1)
                    sp.dma_start(dft_tab[:, :, :, :], a["c_dft"]).then_inc(s_small, 16)
                    sp.dma_start(dft_ch[:, :], a["c_dft_ch"]).then_inc(s_small, 16)
                    sp.dma_start(dft_pr[:, :, :], a["c_dft_pr"]).then_inc(s_small, 16)
                    sp.dma_start(rope[:, :, :, :], a["c_rope"]).then_inc(s_small, 16)
                    kg = a["cache_gqa_k"][0, layer]
                    for dup in range(2):
                        sp.dma_start(k_cache[:, 0:2, dup * HD:(dup + 1) * HD], kg).then_inc(s_kc, 16)
                    sp.dma_start(k_cache[:, 2:6, :], a["cache_diff_k"][0, layer].rearrange("n h m d -> n h (m d)")).then_inc(s_kc, 16)
                    sp.dma_start(v_tok[:, 0, 0:P], a["cache_gqa_v"][0, layer].rearrange("n h d -> n (h d)")).then_inc(s_cv, 16)
                    sp.dma_start(v_tok[:, 0, P:640], a["cache_diff_v"][0, layer].rearrange("n h d -> n (h d)")).then_inc(s_cv, 16)
                    for i in range(2, N_WIN + 4):
                        stream(i)
                    sp.wait_ge(s_rope, n_x[(CH_KVG, 0)] + 1)
                    sp.dma_start(a["new_gqa_k"][0, layer].rearrange("n h d -> n (h d)"), k_out_g[:, :]).then_inc(s_store, 16)
                    sp.wait_ge(s_free, unit_no[("z", CH_VD + 1, 0)] + 1)
                    sp.dma_start(a["new_diff_k"][0, layer].rearrange("n h m d -> n (h m d)"), k_out_d[:, :]).then_inc(s_store, 16)
                    sp.dma_start(a["new_gqa_v"][0, layer].rearrange("n h d -> n (h d)"), v_tok[:, 5, 0:P]).then_inc(s_store, 16)
                    sp.dma_start(a["new_diff_v"][0, layer].rearrange("n h d -> n (h d)"), v_tok[:, 5, P:640]).then_inc(s_store, 16)
                    for n in range(12):
                        m, b = divmod(n, 3)
                        if n >= 2:
                            sp.wait_ge(g_pfull, 2 * (n - 1))
                        sp.dma_start(pw[n % 2][:, :, :], w_br[b][:, :, m * WC:(m + 1) * WC]).then_inc(p_ld[n % 2], 16)
                        if N_WIN + 4 + n < N_STREAM:
                            stream(N_WIN + 4 + n)
                    sp.wait_ge(s_store, 16 * 4)

                @block.gpsimd
                def _(pool):
                    def lo(i):
                        pool.wait_ge(w_hi, i + 1)
                        pool.tensor_tensor(wlo[i % 2][:, :, :], raw[i % 2][:, :, :], whi[i % 2][:, :, :].bitcast(F32),
                                           ALU.subtract).then_inc(w_lo, 1)
                    lo(0)
                    lo(1)
                    norm_pool(pool, nb_mix)
                    for i in range(2, N_WIN + 2):
                        lo(i)
                    for m in range(4):
                        for b in range(3):
                            if N_WIN + 3 * m + b + 2 < N_STREAM:
                                lo(N_WIN + 3 * m + b + 2)
                        for fc in range(2):
                            pool.wait_ge(g_hi, 2 * m + fc + 1)
                            pool.tensor_tensor(mg_lo[:, 2 * m + fc, :], mg[:, fc, :], mg_hi[:, 2 * m + fc, :].bitcast(F32),
                                               ALU.subtract).then_inc(g_lo, 1)
                    for i in range(N_WIN + 14, N_STREAM):
                        lo(i)

                @block.scalar
                def _(act):
                    def hi(i):
                        act.wait_ge(w_ld[i % 2], 16 * (i // 2 + 1))
                        act.activation(whi[i % 2][:, :, :], raw[i % 2][:, :, :], ACT.Copy).then_inc(w_hi, 1)

                    hi(0)
                    hi(1)
                    norm_act_squares(act, nb_mix)
                    norm_act_modulate(act, nb_mix, mul1, shift1)
                    n_sqrt = 0
                    for n, u in enumerate(units):
                        act.wait_ge(s_full, n + 1)
                        if u[0] == "u":
                            act.activation(u_T[:, u[1], :].rearrange("p (a b) -> p a b", a=2), pair(n)[:, :, 0:HALF],
                                           ACT.Copy).then_inc(s_free, 1)
                            if u[1] % 2 == 1:
                                hi(u[1] // 2 + 2)
                        elif u[0] == "ab":
                            g, part = u[1:]
                            t0, t1 = ((0, 4), (4, 5))[part]
                            act.activation(ab[:, g % 2, t0:t1, :].rearrange("p t c -> p (t c)"),
                                           flat(n)[:, 0:(t1 - t0) * 2 * P], ACT.Copy).then_inc(s_free, 1)
                        elif u[0] == "y":
                            act.activation(y_T[:, u[1], 0:P], pair(n)[:, 0, 0:P], ACT.Copy)
                            act.activation(y_T[:, u[1], P:TOK], pair(n)[:, 1, :], ACT.Copy).then_inc(s_free, 1)
                        elif u[0] == "kcache":
                            act.activation(k_T[:, :, 0:P], flat(n)[:, 0:6 * P].rearrange("p (c k) -> p c k", c=6),
                                           ACT.Copy).then_inc(s_free, 1)
                        elif u[0] == "z":
                            c, t = u[1:]
                            if c < CH_VD:
                                i = n_x[(c, t)]
                                if i >= 4:
                                    act.wait_ge(s_rope, i - 3)
                            if c == CH_KVG:
                                act.activation(v_tok[:, key_tile(t), 0:P], flat(n)[:, P:2 * P], ACT.Copy)
                                act.activation(z_s[:, i % 4, 0:P], flat(n)[:, 0:P], ACT.Copy).then_inc(s_free, 1)
                            elif c >= CH_VD:
                                c0 = P + (c - CH_VD) * WC
                                act.activation(v_tok[:, key_tile(t), c0:c0 + WC], flat(n)[:, 0:WC], ACT.Copy).then_inc(s_free, 1)
                            else:
                                if c in (CH_KD, CH_KD + 1) and t == 0:
                                    c0 = (c - CH_KD) * WC
                                    act.activation(k_out_d[:, c0:c0 + WC], flat(n)[:, 0:WC], ACT.Copy)
                                act.activation(z_s[:, i % 4, :], flat(n)[:, 0:WC], ACT.Copy).then_inc(s_free, 1)
                            if c < CH_QD:
                                w = P if c == CH_KVG else WC
                                if n_sqrt:
                                    act.wait_ge(s_vs, 3 * n_sqrt)
                                act.wait_ge(s_free, n + 1)
                                act.activation(z_q[:, 0:w], z_s[:, i % 4, 0:w], ACT.Square).then_inc(s_vs, 1)
                                act.wait_ge(s_vs, 3 * n_sqrt + 3)
                                act.activation(z_d[:, 0:w // HD], z_v[:, 0:w // HD], ACT.Sqrt).then_inc(s_va, 1)
                                n_sqrt += 1
                            if t == TT - 1 and c + 2 <= CH_GATE + 1:
                                hi(c + 2)
                        else:
                            c, t = u[1:]
                            kt = key_tile(t)
                            src = flat(n)[:, 0:WC].rearrange("p (c k) -> p c k", c=2)
                            if c in (CH_QG, CH_QG + 1, CH_QD, CH_QD + 1):
                                q0 = 2 * (c - CH_QG) if c < CH_QD else 4 + 2 * (c - CH_QD)
                                act.activation(q_T[:, q0:q0 + 2, t * P:(t + 1) * P], src, ACT.Copy,
                                               scale=SCALE).then_inc(s_free, 1)
                            else:
                                k0 = 0 if c == CH_KVG else 2 + 2 * (c - CH_KD)
                                act.activation(k_T[:, k0:k0 + 2, kt * P:(kt + 1) * P], src, ACT.Copy).then_inc(s_free, 1)

                    def exps(i):
                        for n in range(first_map[i], map_end[i]):
                            t = maps[n][2]
                            act.wait_ge(t_max, n + 1)
                            if n >= 4:
                                act.wait_ge(t_tr, max(j for j in range(len(att)) if first_map[j] <= n - 4) + 1)
                            act.activation(prob_view(n, t), scores_view(n, t), ACT.Exp, bias=small[:, n % 4, 0:1],
                                           accum_out=small[:, n % 4, 1:2]).then_inc(t_exp, 1)

                    def keep_T(i):
                        w = P * len(key_tiles(att[i][2]))
                        act.wait_ge(t_tr, i + 1)
                        if i >= 2:
                            act.wait_ge(t_pv, i - 1)
                        act.activation(prob_T[:, i % 2, :, :].rearrange("p t q -> p (t q)")[:, 0:w], flat(2)[:, 0:w],
                                       ACT.Copy).then_inc(t_pt, 1)

                    for i in range(len(att) + 3):
                        if i < len(att):
                            exps(i)
                        if 2 <= i < len(att) + 2:
                            keep_T(i - 2)
                    act.wait_ge(t_o, len(att))
                    for j in range(TT * DH):
                        t, h = divmod(j, DH)
                        if j >= 4:
                            act.wait_ge(d_sq, j - 3)
                        act.activation(prob[:, j % 4, 0:P], od[:, t, h, :], ACT.Square,
                                       accum_out=od_ss[:, j:j + 1]).then_inc(d_sq, 1)
                    act.wait_ge(d_1, 1)
                    act.activation(od_r[:, :], od_ss[:, :], ACT.Sqrt).then_inc(d_2, 1)
                    for h in range(DH):
                        act.wait_ge(d_t, h + 1)
                        act.activation(q_T[:, 4 + h, :], flat(h)[:, 0:TOK], ACT.Copy,
                                       scale=sub_gain[:, 0:1]).then_inc(d_k, 1)
                    for m in range(4):
                        for b in range(3):
                            for fc in range(2):
                                g = 6 * m + 2 * b + fc
                                act.wait_ge(g_full, g + 1)
                                if g >= 2:
                                    act.wait_ge(g_pfree, g - 1)
                                act.activation(sig_m[:, g % 2, :].rearrange("p (a b) -> p a b", a=2),
                                               pair(g % 2)[:, :, 0:HALF], ACT.Sigmoid).then_inc(g_sig, 1)
                            if N_WIN + 3 * m + b + 2 < N_STREAM:
                                hi(N_WIN + 3 * m + b + 2)
                        for fc in range(2):
                            act.wait_ge(g_acc, 4 * (m + 1))
                            act.activation(mg_hi[:, 2 * m + fc, :], mg[:, fc, :], ACT.Copy).then_inc(g_hi, 1)
                    for i in range(N_WIN + 14, N_STREAM):
                        act.wait_ge(o_full, 2 * (i - 2 - N_WIN - 12) + 2)
                        hi(i)

                @block.vector
                def _(dve):
                    norm_dve(dve, nb_mix, n_lo)
                    dve.wait_ge(s_small, 16 * 4)
                    n_rope = [0]

                    def step(ins):
                        n_rope[0] += 1
                        ins.then_inc(s_r, 1)
                        dve.wait_ge(s_r, n_rope[0])

                    n_sqrt = 0
                    for i, (c, t) in enumerate(turned):
                        zn = unit_no[("z", c, t)]
                        w = P if c == CH_KVG else WC
                        nh = w // HD
                        zin = z_s[:, i % 4, 0:w]
                        heads = zin.rearrange("p (h d) -> p h d", d=HD)
                        dve.wait_ge(s_free, zn + 1)
                        if i >= 1:
                            dve.wait_ge(s_rope, i)
                        if i >= 4:
                            dve.wait_ge(s_full, unit_no[("x",) + turned[i - 4]] + 1)
                        if is_gqa(c):
                            dve.wait_ge(s_vs, 3 * n_sqrt + 1)
                            dve.tensor_reduce(z_ss[:, 0:nh], z_q[:, 0:w].rearrange("p (h d) -> p h d", d=HD),
                                              AX.X, ALU.add).then_inc(s_vs, 1)
                            dve.wait_ge(s_vs, 3 * n_sqrt + 2)
                            dve.tensor_scalar(z_v[:, 0:nh], z_ss[:, 0:nh], 1.0 / HD, EPS, ALU.mult, ALU.add).then_inc(s_vs, 1)
                            dve.wait_ge(s_va, n_sqrt + 1)
                            step(dve.reciprocal(z_i[:, 0:nh], z_d[:, 0:nh]))
                            step(dve.tensor_tensor(heads, heads, z_i[:, 0:nh].unsqueeze(2).to_broadcast([P, nh, HD]), ALU.mult))
                            gain = qk_gain[:, 1 if c == CH_KVG else 0, :].unsqueeze(1).to_broadcast([P, nh, HD])
                            step(dve.tensor_tensor(heads, heads, gain, ALU.mult))
                            n_sqrt += 1
                        if c == CH_KVG:
                            dst = z_r[:, i % 4, :].rearrange("p (h u d) -> p h u d", h=2, u=2)
                            outs = [dst[:, :, 0, :], dst[:, :, 1, :]]
                        else:
                            outs = [z_r[:, i % 4, :].rearrange("p (h d) -> p h d", d=HD)]
                        if t == 0:
                            if c == CH_KVG:
                                dve.tensor_copy(k_out_g[:, :], zin)
                                dve.tensor_copy(outs[1], heads)
                            dve.tensor_copy(outs[0], heads).then_inc(s_rope, 1)
                            continue
                        cos = rope[:, 0, t - 1, :].unsqueeze(1).to_broadcast([P, nh, HD])
                        halves = zin.rearrange("p (h a b d) -> p h a b d", a=2, b=2, d=16)
                        turned_h = z_t[:, 0:w].rearrange("p (h a b d) -> p h a b d", a=2, b=2, d=16)
                        sin = rope[:, 1, t - 1, :].rearrange("p (a b d) -> p a b d", a=2, b=2)
                        for hb in range(2):
                            s_bc = sin[:, :, hb, :].unsqueeze(1).to_broadcast([P, nh, 2, 16])
                            dve.tensor_tensor(turned_h[:, :, :, hb, :], halves[:, :, :, 1 - hb, :], s_bc, ALU.mult).then_inc(s_r, 1)
                        dve.tensor_tensor(outs[0], heads, cos, ALU.mult).then_inc(s_r, 1)
                        n_rope[0] += 3
                        dve.wait_ge(s_r, n_rope[0])
                        tv = z_t[:, 0:w].rearrange("p (h d) -> p h d", d=HD)
                        if c == CH_KVG:
                            step(dve.tensor_tensor(outs[0], outs[0], tv, ALU.add))
                            dve.tensor_copy(outs[1], outs[0]).then_inc(s_rope, 1)
                        else:
                            dve.tensor_tensor(outs[0], outs[0], tv, ALU.add).then_inc(s_rope, 1)

                    def maxima(i):
                        for n in range(first_map[i], map_end[i]):
                            t = maps[n][2]
                            dve.wait_ge(t_s, n + 1)
                            if n >= 4:
                                dve.wait_ge(t_p, max(j for j in range(len(att)) if first_map[j] <= n - 4) + 1)
                            dve.tensor_reduce(small[:, n % 4, 0:1], scores_view(n, t), AX.X if t == 0 else AX.XY,
                                              ALU.max, negate=True).then_inc(t_max, 1)

                    n_inv = [0]

                    def normalise(i):
                        kind, h, t = att[i]
                        n = first_map[i]
                        w = P if t == 0 else KEYS
                        dve.wait_ge(t_exp, map_end[i])
                        for j in range(n, map_end[i]):
                            dve.reciprocal(small[:, j % 4, 2:3], small[:, j % 4, 1:2]).then_inc(t_l, 1)
                            n_inv[0] += 1
                        dve.wait_ge(t_l, n_inv[0])
                        p0 = prob[:, n % 4, 0:w]
                        if kind == "g":
                            dve.tensor_scalar(p0, p0, small[:, n % 4, 2:3], None, ALU.mult).then_inc(t_p, 1)
                            return
                        p1 = prob[:, (n + 1) % 4, 0:w]
                        dve.tensor_scalar(p0, p0, small[:, n % 4, 2:3], None, ALU.mult).then_inc(t_l, 1)
                        dve.tensor_scalar(small[:, n % 4, 3:4], small[:, (n + 1) % 4, 2:3], neg_lam[:, 0:1], None,
                                          ALU.mult).then_inc(t_l, 1)
                        n_inv[0] += 2
                        dve.wait_ge(t_l, n_inv[0])
                        dve.scalar_tensor_tensor(out=p0, in0=p1, scalar=small[:, n % 4, 3:4], in1=p0,
                                                 op0=ALU.mult, op1=ALU.add).then_inc(t_p, 1)

                    def keep_o(i):
                        kind, h, t = att[i]
                        bank = psum[:, 6 + i % 2, 0:P]
                        if att[i] == ("d", 0, 0):
                            dve.wait_ge(s_store, 16 * 4)
                        dve.wait_ge(t_pv, i + 1)
                        if kind == "g":
                            r = HD * (h % 2)
                            dve.tensor_copy(q_T[r:r + HD, h // 2, t * P:(t + 1) * P], bank[r:r + HD, :]).then_inc(t_o, 1)
                        else:
                            dve.tensor_copy(od[:, t, h, :], bank).then_inc(t_o, 1)

                    for i in range(len(att) + 3):
                        if i < len(att):
                            maxima(i)
                        if 1 <= i < len(att) + 1:
                            normalise(i - 1)
                        if i >= 3:
                            keep_o(i - 3)
                    dve.wait_ge(d_sq, TT * DH)
                    dve.tensor_scalar(od_ss[:, :], od_ss[:, :], 1.0 / (2 * HD), EPS, ALU.mult, ALU.add).then_inc(d_1, 1)
                    dve.wait_ge(d_2, 1)
                    dve.reciprocal(od_ss[:, :], od_r[:, :]).then_inc(d_1, 1)
                    dve.wait_ge(d_1, 2)
                    for h in range(DH):
                        rs = od_ss[:, :].rearrange("p (t h) -> p t h", h=DH)[:, :, h]
                        dve.tensor_tensor(od[:, :, h, :], od[:, :, h, :], rs.unsqueeze(2).to_broadcast([P, TT, P]),
                                          ALU.mult).then_inc(d_3, 1)
                    n_acc = 0
                    for m in range(4):
                        for b in range(3):
                            for fc in range(2):
                                g = 6 * m + 2 * b + fc
                                dve.wait_ge(g_sig, g + 1)
                                dve.wait_ge(g_pfull, g + 1)
                                src = pair(2 + g % 2)[:, :, 0:HALF]
                                sg = sig_m[:, g % 2, :].rearrange("p (a b) -> p a b", a=2)
                                if b == 0:
                                    if m >= 1:
                                        dve.wait_ge(g_lo, 2 * m)
                                    dst = mg[:, fc, :]
                                else:
                                    dst = mg_t[:, :]
                                dve.tensor_tensor(dst.rearrange("p (a b) -> p a b", a=2), src, sg, ALU.mult).then_inc(g_pfree, 1)
                                if b > 0:
                                    dve.wait_ge(g_pfree, g + 1)
                                    dve.tensor_tensor(mg[:, fc, :], mg[:, fc, :], mg_t[:, :], ALU.add).then_inc(g_acc, 1)
                                    n_acc += 1
                                    dve.wait_ge(g_acc, n_acc)
                    for f in range(KD):
                        dve.wait_ge(o_full, f + 1)
                        add_gated(dve, f, pair(f), gate1, o_add)

                @block.tensor
                def _(pe):
                    norm_pe(pe, nb_mix)

                    def feature_major(dst, i, fc, mv_hi, mv_lo, waits=None):
                        for kc in range(KD):
                            if waits is not None:
                                pe.wait_ge(waits, kc + 1)
                            cs = slice(fc * P, (fc + 1) * P)
                            mm = mm_split(pe, [dst[:, 0, 0:HALF], dst[:, 1, 0:HALF]],
                                          whi[i % 2][:, kc, cs], wlo[i % 2][:, kc, cs],
                                          [mv_hi[:, kc, 0:HALF], mv_hi[:, kc, HALF:TOK]],
                                          [mv_lo[:, kc, 0:HALF], mv_lo[:, kc, HALF:TOK]], kc == 0, kc == KD - 1)
                        return mm

                    for n, u in enumerate(units):
                        if n >= 4:
                            pe.wait_ge(s_free, n - 3)
                        if u[0] == "u":
                            g = u[1]
                            pe.wait_ge(w_lo, g // 2 + 1)
                            mm = feature_major(pair(n), g // 2, g % 2, h_hi, h_lo, n_lo if g == 0 else None)
                            mm.then_inc(s_full, 1)
                        elif u[0] == "ab":
                            g, part = u[1:]
                            if (g, part) == (0, 0):
                                pe.wait_ge(s_small, 16 * 4)
                            pe.wait_ge(s_free, unit_no[("u", g)] + 1)
                            for t in ((0, 1, 2, 3), (4,))[part]:
                                mm = pe.matmul(flat(n)[:, (t % 4) * 2 * P:(t % 4 + 1) * 2 * P], u_T[:, g, t * P:(t + 1) * P],
                                               dft_ch[:, :], start=True, stop=True)
                            mm.then_inc(s_full, 1)
                        elif u[0] == "y":
                            g = u[1]
                            pe.wait_ge(s_free, unit_no[("ab", g, 1)] + 1)
                            for part in range(2):
                                pe.matmul(pair(n)[:, 0, 0:P], ab[:, g % 2, 0, part * P:(part + 1) * P], dft_pr[:, part, :],
                                          start=(part == 0), stop=(part == 1))
                            for t in range(4):
                                for part in range(2):
                                    mm = pe.matmul(pair(n)[:, 1, :], ab[:, g % 2, t + 1, part * P:(part + 1) * P],
                                                   dft_tab[:, part, t, :], start=(t == 0 and part == 0),
                                                   stop=(t == 3 and part == 1))
                            mm.then_inc(s_full, 1)
                        elif u[0] == "kcache":
                            pe.wait_ge(s_kc, 48)
                            for c in range(6):
                                mm = pe.transpose(flat(n)[:, c * P:(c + 1) * P], k_cache[:, c, :], ident[:, :])
                            mm.then_inc(s_full, 1)
                        elif u[0] == "z":
                            c, t = u[1:]
                            pe.wait_ge(w_lo, c + 1)
                            ts = slice(t * P, (t + 1) * P)
                            for kc in range(KD):
                                mm = mm_split(pe, [flat(n)[:, 0:WC]], h_hi[:, kc, ts], h_lo[:, kc, ts],
                                              [whi[c % 2][:, kc, :]], [wlo[c % 2][:, kc, :]], kc == 0, kc == KD - 1)
                            mm.then_inc(s_full, 1)
                        else:
                            c, t = u[1:]
                            i = n_x[(c, t)]
                            pe.wait_ge(s_rope, i + 1)
                            for q in range(2):
                                mm = pe.transpose(flat(n)[:, q * P:(q + 1) * P], z_r[:, i % 4, q * P:(q + 1) * P], ident[:, :])
                            mm.then_inc(s_full, 1)

                    def scores(i):
                        for n in range(first_map[i], map_end[i]):
                            kind, h, t, m = maps[n]
                            if n >= 2:
                                pe.wait_ge(t_exp, n - 1)
                            if t == 0:
                                mm = pe.matmul(flat(n % 2)[:, 0:P], q_slice(kind, h, t, m), k_slice(kind, h, m, 5 * P, 6 * P),
                                               start=True, stop=True)
                            else:
                                for hf in range(2):
                                    mm = pe.matmul(pair(n % 2)[:, hf, 0:HALF], q_slice(kind, h, t, m),
                                                   k_slice(kind, h, m, hf * HALF, (hf + 1) * HALF), start=True, stop=True)
                            mm.then_inc(t_s, 1)

                    def turn(i):
                        pe.wait_ge(t_p, i + 1)
                        if i >= 1:
                            pe.wait_ge(t_pt, i)
                        for j in range(len(key_tiles(att[i][2]))):
                            mm = pe.transpose(flat(2)[:, j * P:(j + 1) * P], prob[:, first_map[i] % 4, j * P:(j + 1) * P],
                                              ident[:, :])
                        mm.then_inc(t_tr, 1)

                    def values(i):
                        kind, h, t = att[i]
                        tiles = key_tiles(t)
                        pe.wait_ge(t_pt, i + 1)
                        if i == 0:
                            pe.wait_ge(s_cv, 32)
                        if i >= 2:
                            pe.wait_ge(t_o, i - 1)
                        for j, kt in enumerate(tiles):
                            st, sp_ = j == 0, j == len(tiles) - 1
                            if kind == "g":
                                r = HD * (h % 2)
                                v0 = HD * (h // (QH // KVH))
                                mm = pe.matmul(psum[r:r + HD, 6 + i % 2, 0:P], v_tok[:, kt, v0:v0 + HD],
                                               prob_T[:, i % 2, j, :], start=st, stop=sp_)
                            else:
                                mm = pe.matmul(psum[:, 6 + i % 2, 0:P], prob_T[:, i % 2, j, :],
                                               v_tok[:, kt, P + h * P:P + (h + 1) * P], start=st, stop=sp_)
                        mm.then_inc(t_pv, 1)

                    pe.wait_ge(s_free, len(units))
                    for i in range(len(att) + 3):
                        if i < len(att):
                            scores(i)
                        if 2 <= i < len(att) + 2:
                            turn(i - 2)
                        if i >= 3:
                            values(i - 3)
                    for h in range(DH):
                        pe.wait_ge(d_3, h + 1)
                        if h == 2:
                            pe.wait_ge(t_pt, len(att))
                        if h == 3:
                            pe.wait_ge(t_o, len(att))
                        for t in range(TT):
                            mm = pe.transpose(flat(h)[:, t * P:(t + 1) * P], od[:, t, h, :], ident[:, :])
                        mm.then_inc(d_t, 1)
                    pe.wait_ge(d_k, DH)
                    branch = (y_T, q_T[:, 0:4, :], q_T[:, 4:8, :])
                    for m in range(4):
                        for b in range(3):
                            i = N_WIN + 3 * m + b
                            n_p = 3 * m + b
                            pe.wait_ge(w_lo, i + 1)
                            for fc in range(2):
                                g = 6 * m + 2 * b + fc
                                if g >= 2:
                                    pe.wait_ge(g_sig, g - 1)
                                mm = feature_major(pair(g % 2), i, fc, h_hi, h_lo)
                                mm.then_inc(g_full, 1)
                                pe.wait_ge(p_ld[n_p % 2], 16 * (n_p // 2 + 1))
                                if g >= 2:
                                    pe.wait_ge(g_pfree, g - 1)
                                for kc in range(4):
                                    for hf in range(2):
                                        mm = pe.matmul(pair(2 + g % 2)[:, hf, 0:HALF], pw[n_p % 2][:, kc, fc * P:(fc + 1) * P],
                                                       branch[b][:, kc, hf * HALF:(hf + 1) * HALF],
                                                       start=(kc == 0), stop=(kc == 3))
                                mm.then_inc(g_pfull, 1)
                    pe.wait_ge(g_pfree, 24)
                    pe.wait_ge(g_sig, 24)
                    for f in range(KD):
                        i = N_WIN + 12 + f // 2
                        pe.wait_ge(w_lo, i + 1)
                        if f == 0:
                            pe.wait_ge(g_lo, KD)
                        if f >= 4:
                            pe.wait_ge(o_add, f - 3)
                        feature_major(pair(f), i, f % 2, mg_hi, mg_lo).then_inc(o_full, 1)
            clear()

            with nc.Block() as block:
                @block.sync
                def _(sp):
                    src = {"g": a["w_e_gate"][layer], "u": a["w_e_up"][layer], "d": a["w_e_down"][layer]}

                    def load(r, e):
                        w = src[r][e].rearrange("(k p) n -> p k n", p=P)
                        sp.dma_start(ex[r][0][:, :, :], w).then_inc(x_ld[r], 16)

                    def load_combine(e):
                        sp.dma_start(cb[:, 0, :], comb_dram[e].partition_broadcast(P)).then_inc(c_ld, 16)

                    load("g", 0)
                    load("u", 0)
                    load("d", 0)
                    sp.wait_ge(r_ce, 1)
                    sp.dma_start(comb_dram, comb_T[:, :]).then_inc(r_cs, 16)
                    sp.wait_ge(r_cs, 16)
                    load_combine(0)
                    with sp.Fori(1, NE) as e:
                        for r in "gud":
                            sp.wait_ge(x_lo[r], e)
                            load(r, e)
                            if r == "u":
                                sp.wait_ge(x_sg, 2 * e)
                                load_combine(e)

                @block.gpsimd
                def _(pool):
                    pool.memset(y_acc[:, :, :], 0.0).then_inc(x_y0, 1)

                    def lo(r, e):
                        pool.wait_ge(x_hi[r], e + 1)
                        pool.tensor_tensor(ex[r][2][:, :, :], ex[r][0][:, :, :], ex[r][1][:, :, :].bitcast(F32),
                                           ALU.subtract).then_inc(x_lo[r], 1)

                    def act_low(e):
                        pool.wait_ge(x_ahi, e + 1)
                        pool.tensor_tensor(act_lo[:, :, :], act_f[:, :, :], act_hi[:, :, :].bitcast(F32),
                                           ALU.subtract).then_inc(x_alo, 1)
                    lo("g", 0)
                    lo("u", 0)
                    norm_pool(pool, nb_moe)
                    lo("g", 1)
                    lo("u", 1)

                    def body(e, last=False):
                        act_low(e - 1)
                        lo("d", e - 1)
                        if not last:
                            lo("g", e + 1)
                            lo("u", e + 1)
                    with pool.Fori(1, NE - 1) as e:
                        body(e)
                    body(NE - 1, last=True)
                    act_low(NE - 1)
                    lo("d", NE - 1)

                @block.scalar
                def _(act):
                    def hi(r, e, used=None):
                        act.wait_ge(x_ld[r], 16 * (e + 1))
                        if used is not None:
                            act.wait_ge(x_full, used)
                        act.activation(ex[r][1][:, :, :], ex[r][0][:, :, :], ACT.Copy).then_inc(x_hi[r], 1)

                    def sigmoid(e, fc):
                        act.wait_ge(x_full, 12 * e - 8 + fc + 1)
                        act.activation(sig_x[:, fc, :].rearrange("p (a b) -> p a b", a=2), pair(fc)[:, :, 0:HALF],
                                       ACT.Sigmoid).then_inc(x_sig, 1)

                    def act_high(e, kept, used=None):
                        act.wait_ge(x_free, kept)
                        if used is not None:
                            act.wait_ge(x_full, used)
                        act.activation(act_hi[:, :, :], act_f[:, :, :], ACT.Copy).then_inc(x_ahi, 1)

                    hi("g", 0)
                    hi("u", 0)
                    norm_act_squares(act, nb_moe)
                    norm_act_modulate(act, nb_moe, mul2, shift2)
                    act.wait_ge(r_lg, 1)
                    act.activation(sc[:, :], psum[:, 4, 0:TT * NE], ACT.Sigmoid).then_inc(r_sg, 1)
                    for fc in range(2):
                        act.wait_ge(x_full, fc + 1)
                        act.activation(sig_x[:, fc, :].rearrange("p (a b) -> p a b", a=2), pair(fc)[:, :, 0:HALF],
                                       ACT.Sigmoid).then_inc(x_sig, 1)
                    act.wait_ge(r_ct, 1)
                    act.activation(comb_T[:, :], flat(2)[0:NE, 0:TOK], ACT.Copy).then_inc(r_ce, 1)
                    hi("g", 1, 2)
                    hi("u", 1, 4)

                    def body(e, last=False):
                        u0 = 12 * e - 8
                        one = isinstance(e, int) and e == 1
                        act_high(e - 1, 4 if one else u0 - 8, None if one else u0)
                        hi("d", e - 1, None if one else u0)
                        for fc in range(2):
                            sigmoid(e, fc)
                        if not last:
                            hi("g", e + 1, u0 + 2)
                            hi("u", e + 1, u0 + 4)
                    body(1)
                    with act.Fori(2, NE - 1) as e:
                        body(e)
                    body(NE - 1, last=True)
                    act_high(NE - 1, 12 * NE - 16, 12 * NE - 8)
                    hi("d", NE - 1, 12 * NE - 8)

                @block.vector
                def _(dve):
                    norm_dve(dve, nb_moe, n_lo)
                    n_st = [0]

                    def step(ins):
                        n_st[0] += 1
                        ins.then_inc(r_st, 1)
                        dve.wait_ge(r_st, n_st[0])

                    def ranks(dst, v, n):
                        jj = v.unsqueeze(3).to_broadcast([P, n, 4, 4])
                        ii = v.unsqueeze(2).to_broadcast([P, n, 4, 4])
                        gt = cmp_gt[:, 0:n * 16].rearrange("p (n j i) -> p n j i", j=4, i=4)
                        eq = cmp_eq[:, 0:n * 16].rearrange("p (n j i) -> p n j i", j=4, i=4)
                        step(dve.tensor_tensor(gt, ii, jj, ALU.is_gt))
                        step(dve.tensor_tensor(eq, ii, jj, ALU.is_equal))
                        step(dve.tensor_tensor(eq.rearrange("p n j i -> p n (j i)"), eq.rearrange("p n j i -> p n (j i)"),
                                               tie[:, :, :].rearrange("p j i -> p (j i)").unsqueeze(1).to_broadcast([P, n, 16]),
                                               ALU.mult))
                        step(dve.tensor_tensor(cmp_gt[:, 0:n * 16], cmp_gt[:, 0:n * 16], cmp_eq[:, 0:n * 16], ALU.add))
                        step(dve.tensor_reduce(dst, gt.rearrange("p n j i -> p (n j) i"), AX.X, ALU.add))

                    dve.wait_ge(r_sg, 1)
                    e3 = lambda x: x[:, :].rearrange("p (t e) -> p t e", e=NE)
                    step(dve.tensor_tensor(e3(sel), e3(sc), bias_bc[:, :].unsqueeze(1).to_broadcast([P, TT, NE]), ALU.add))
                    ranks(rank[:, :], sel[:, :].rearrange("p (n j) -> p n j", j=4), TT * NG)
                    step(dve.tensor_scalar(top2[:, :], rank[:, :], 1.5, None, ALU.is_lt))
                    step(dve.tensor_tensor(tmp16[:, :], top2[:, :], sel[:, :], ALU.mult))
                    step(dve.tensor_reduce(grp[:, :], tmp16[:, :].rearrange("p (n j) -> p n j", j=4), AX.X, ALU.add))
                    ranks(grank[:, :], grp[:, :].rearrange("p (n j) -> p n j", j=4), TT)
                    step(dve.tensor_scalar(gbest[:, :], grank[:, :], 0.5, None, ALU.is_lt))
                    g3 = lambda x: x[:, :].rearrange("p (n j) -> p n j", j=4)
                    step(dve.tensor_tensor(g3(top2), g3(top2), gbest[:, :].unsqueeze(2).to_broadcast([P, TT * NG, 4]), ALU.mult))
                    step(dve.tensor_tensor(tmp16[:, :], top2[:, :], sc[:, :], ALU.mult))
                    step(dve.tensor_reduce(wsum[:, :], e3(tmp16), AX.X, ALU.add))
                    step(dve.reciprocal(wrec[:, :], wsum[:, :]))
                    step(dve.tensor_tensor(e3(comb), e3(tmp16), wrec[:, :].unsqueeze(2).to_broadcast([P, TT, NE]), ALU.mult))
                    dve.wait_ge(x_y0, 1)

                    def halves(v):
                        return v.rearrange("p (a b) -> p a b", a=2)

                    def gated(e, fc):
                        dve.wait_ge(x_sig, 2 * e + fc + 1)
                        dve.tensor_tensor(halves(sig_x[:, fc, :]), pair(fc)[:, :, 0:HALF], halves(sig_x[:, fc, :]),
                                          ALU.mult).then_inc(x_free, 1)

                    def combined(e, fc, free):
                        dve.wait_ge(c_ld, 16 * (e + 1))
                        dve.wait_ge(x_free, free)
                        ins = dve.tensor_tensor(sig_x[:, fc, :], sig_x[:, fc, :], cb[:, 0, :], ALU.mult).then_inc(x_sg, 1)
                        return ins

                    def activated(e, fc, full):
                        dve.wait_ge(x_full, full)
                        dve.wait_ge(x_sg, 2 * e + fc + 1)
                        dve.tensor_tensor(halves(act_f[:, fc, :]), pair(2 + fc)[:, :, 0:HALF], halves(sig_x[:, fc, :]),
                                          ALU.mult).then_inc(x_free, 1)

                    def down(u0):
                        for f in range(KD):
                            dve.wait_ge(x_full, u0 + f + 1)
                            dve.tensor_tensor(halves(y_acc[:, f, :]), pair(f)[:, :, 0:HALF], halves(y_acc[:, f, :]),
                                              ALU.add).then_inc(x_free, 1)

                    def expert(e, u0):
                        gated(e, 0)
                        gated(e, 1)
                        combined(e, 0, u0 + 1)
                        combined(e, 1, u0 + 2)
                        activated(e, 0, u0 + 3)
                        activated(e, 1, u0 + 4)

                    expert(0, 0)
                    with dve.Fori(1, NE) as e:
                        dve.wait_ge(x_alo, e)
                        expert(e, 12 * e - 8)
                        down(12 * e - 4)
                    down(12 * NE - 8)
                    dve.wait_ge(x_free, 12 * NE)
                    for f in range(KD):
                        for s, (c0, c1) in enumerate(((0, N_PROMPT), (N_PROMPT, TOK))):
                            dve.scalar_tensor_tensor(out=x_T[:, f, c0:c1], in0=y_acc[:, f, c0:c1], scalar=gate2[:, f, s:s + 1],
                                                     in1=x_T[:, f, c0:c1], op0=ALU.mult, op1=ALU.add).then_inc(x_step, 1)

                @block.tensor
                def _(pe):
                    norm_pe(pe, nb_moe)
                    pe.wait_ge(n_lo, KD)
                    for t in range(TT):
                        ts = slice(t * P, (t + 1) * P)
                        for kc in range(KD):
                            for n, (hp, wp) in enumerate(((h_hi, wr_hi), (h_hi, wr_lo), (h_lo, wr_hi), (h_lo, wr_lo))):
                                mm = pe.matmul(psum[:, 4, t * NE:(t + 1) * NE], hp[:, kc, ts], wp[:, kc, :],
                                               start=(kc == 0 and n == 0), stop=(kc == KD - 1 and n == 3))
                    mm.then_inc(r_lg, 1)

                    def up_or_gate(r, fc, slot, free=None):
                        if free is not None:
                            pe.wait_ge(x_free, free)
                        cs = slice(fc * P, (fc + 1) * P)
                        dst = pair(slot)
                        for kc in range(KD):
                            mm = mm_split(pe, [dst[:, 0, 0:HALF], dst[:, 1, 0:HALF]], ex[r][1][:, kc, cs], ex[r][2][:, kc, cs],
                                          [h_hi[:, kc, 0:HALF], h_hi[:, kc, HALF:TOK]],
                                          [h_lo[:, kc, 0:HALF], h_lo[:, kc, HALF:TOK]], kc == 0, kc == KD - 1)
                        mm.then_inc(x_full, 1)

                    def down(e, u0):
                        pe.wait_ge(x_lo["d"], e + 1)
                        pe.wait_ge(x_alo, e + 1)
                        for f in range(KD):
                            pe.wait_ge(x_free, u0 + f - 3)
                            cs = slice(f * P, (f + 1) * P)
                            dst = pair(f)
                            for kc in range(2):
                                mm = mm_split(pe, [dst[:, 0, 0:HALF], dst[:, 1, 0:HALF]],
                                              ex["d"][1][:, kc, cs], ex["d"][2][:, kc, cs],
                                              [act_hi[:, kc, 0:HALF], act_hi[:, kc, HALF:TOK]],
                                              [act_lo[:, kc, 0:HALF], act_lo[:, kc, HALF:TOK]], kc == 0, kc == 1)
                            mm.then_inc(x_full, 1)

                    pe.wait_ge(x_lo["g"], 1)
                    for fc in range(2):
                        up_or_gate("g", fc, fc)
                    pe.wait_ge(r_st, ROUTE_STEPS)
                    for t in range(TT):
                        mm = pe.transpose(flat(2)[0:NE, t * P:(t + 1) * P], comb[:, t * NE:(t + 1) * NE], ident[:, :])
                    mm.then_inc(r_ct, 1)
                    pe.wait_ge(r_ce, 1)
                    pe.wait_ge(x_lo["u"], 1)
                    for fc in range(2):
                        up_or_gate("u", fc, 2 + fc)
                    with pe.Fori(1, NE) as e:
                        u0 = 12 * e - 8
                        for n, r in enumerate("gu"):
                            pe.wait_ge(x_lo[r], e + 1)
                            for fc in range(2):
                                up_or_gate(r, fc, 2 * n + fc, u0 + 2 * n + fc - 3)
                        down(e - 1, u0 + 4)
                    down(NE - 1, 12 * NE - 8)
            clear()

        y_tok = at("y_tok", [P, 2, D], Z)
        nb_fin = norm_bufs("fin", Z + 20 * K)
        h_fin = at("h_final", [P, KD, TOK], Z + 40 * K)
        f_t, f_e = sem("out_turned"), sem("out_kept")
        f_s = [sem(f"out_stored{i}") for i in range(2)]
        with nc.Block() as block:
            @block.scalar
            def _(act):
                norm_act_squares(act, nb_fin)
                for kc in range(KD):
                    act.wait_ge(n_t, kc + 1)
                    act.activation(h_fin[:, kc, :], nb_fin["h"][:, kc % 2, :], ACT.Copy,
                                   scale=fin_gain[:, kc:kc + 1]).then_inc(n_h, 1)

            @block.vector
            def _(dve):
                norm_dve(dve, nb_fin, n_h)
                for t in range(TT):
                    dve.wait_ge(f_t, t + 1)
                    if t >= 2:
                        dve.wait_ge(f_s[t % 2], 16 * (t // 2))
                    dve.tensor_copy(y_tok[:, t % 2, :], flat(t % 3)[:, :]).then_inc(f_e, 1)

            @block.tensor
            def _(pe):
                norm_pe(pe, nb_fin)
                pe.wait_ge(n_h, KD)
                for t in range(TT):
                    if t >= 3:
                        pe.wait_ge(f_e, t - 2)
                    for kc in range(KD):
                        mm = pe.transpose(flat(t % 3)[:, kc * P:(kc + 1) * P], h_fin[:, kc, t * P:(t + 1) * P], ident[:, :])
                    mm.then_inc(f_t, 1)

            @block.sync
            def _(sp):
                for t in range(TT):
                    sp.wait_ge(f_e, t + 1)
                    dst = a["y_prompt"][0] if t == 0 else a["y_sample"][0, (t - 1) * P:t * P, :]
                    sp.dma_start(dst, y_tok[:, t % 2, :]).then_inc(f_s[t % 2], 16)
                sp.wait_ge(f_s[0], 16 * ((TT + 1) // 2))
                sp.wait_ge(f_s[1], 16 * (TT // 2))


def constants():
    f = np.float32
    c = {"c_ident": np.eye(P, dtype=f), "c_ones": np.ones((P, P), f)}
    j = np.arange(4)
    c["c_tie"] = (j[None, :] < j[:, None]).astype(f)
    init = [0.8 - 0.6 * np.exp(-0.3 * l) for l in range(DEPTH)]
    c["c_lambda"] = np.array([[x, 1.0 - x] for x in init], f)

    def dft(n):
        k = np.arange(n)
        ang = 2 * np.pi * ((k[:, None] * k[None, :]) % n) / n
        return np.cos(ang), -np.sin(ang)
    ch_c, ch_s = dft(FGD)
    c["c_dft_ch"] = np.concatenate([ch_c, ch_s], 1).astype(f)
    sc_, ss_ = dft(N_SAMPLE)
    nrm = 1.0 / np.sqrt(N_SAMPLE * FGD)
    tab = np.stack([sc_ * nrm, -ss_ * nrm])
    c["c_dft"] = np.ascontiguousarray(tab.reshape(2, 4, P, N_SAMPLE).transpose(2, 0, 1, 3)).astype(f)
    pc_, ps_ = dft(N_PROMPT)
    nrm = 1.0 / np.sqrt(N_PROMPT * FGD)
    c["c_dft_pr"] = np.ascontiguousarray(np.stack([pc_ * nrm, -ps_ * nrm], 1)).astype(f)
    grid_w, axis = 64, HD // 2
    pos = np.arange(N_SAMPLE)
    inv = (f(10000.0) ** (-(np.arange(axis // 2, dtype=f) * f(2.0) / f(axis)))).astype(f)
    ar = ((pos // grid_w).astype(f)[:, None] * inv[None, :]).astype(f)
    ac = ((pos % grid_w).astype(f)[:, None] * inv[None, :]).astype(f)
    ang = np.concatenate([ar, ar, ac, ac], -1)
    sign = np.repeat(np.array([-1, 1, -1, 1], f), 16)
    rp = np.stack([np.cos(ang), np.sin(ang) * sign])
    c["c_rope"] = np.ascontiguousarray(rp.reshape(2, 4, P, HD).transpose(2, 0, 1, 3)).astype(f)
    return c


INS = ["x_prompt", "x_sample", "cache_gqa_k", "cache_gqa_v", "cache_diff_k", "cache_diff_v", "c", "c_ctx",
       "norm1_g", "w_mod", "b_mod", "w_in", "gqa_q_norm", "gqa_k_norm", "diff_lambda", "diff_subln_g",
       "w_fourier", "w_gqa_o", "w_diff_o", "w_out", "norm2_g", "w_router", "router_bias", "w_e_gate",
       "w_e_up", "w_e_down", "final_norm_g"]
OUTS = [("y_prompt", (1, N_PROMPT, D)), ("y_sample", (1, N_SAMPLE, D)),
        ("new_gqa_k", (1, DEPTH, N_PROMPT, KVH, HD)), ("new_gqa_v", (1, DEPTH, N_PROMPT, KVH, HD)),
        ("new_diff_k", (1, DEPTH, N_PROMPT, DH, 2, HD)), ("new_diff_v", (1, DEPTH, N_PROMPT, DH, 2 * HD))]


def kernel(**inputs):
    import concourse.bacc as bacc
    from concourse.bass_utils import run_bass_kernel_spmd

    nc = bacc.Bacc("TRN2", target_bir_lowering=False, num_devices=1)
    arrays = {n: np.ascontiguousarray(inputs[n]) for n in INS}
    arrays.update(constants())
    aps = {n: nc.dram_tensor(n, v.shape, F32, kind="ExternalInput").ap() for n, v in arrays.items()}
    for n, shape in OUTS:
        aps[n] = nc.dram_tensor(n, shape, F32, kind="ExternalOutput").ap()
    build(nc, aps)
    r = run_bass_kernel_spmd(nc, [arrays], core_ids=[0])
    return tuple(r.results[0][n] for n, _ in OUTS)
```

```python
from contextlib import ExitStack

import numpy as np
import concourse.bass as bass
from concourse import mybir

F32 = mybir.dt.float32
F32R = mybir.dt.float32r
ALU = mybir.AluOpType
ACT = mybir.ActivationFunctionType
AX = mybir.AxisListType

P = 128
D = 1024
KD = D // P
DEPTH = 2
N_PROMPT, N_SAMPLE, N_PAST = 128, 512, 128
TOK = N_PROMPT + N_SAMPLE
TT = TOK // P
HALF = TOK // 2
KEYS = N_PAST + N_SAMPLE
HD = 64
QH, KVH, DH = 8, 2, 4
FG, FGD = 4, 128
BW = 512
IN_COLS = 2816
WC = 256
NE, NG, EPG = 16, 4, 4
DE = 256
EPS = 1e-6
NH = 3
CH_QG, CH_KVG, CH_QD, CH_KD, CH_VD, CH_GATE = 2, 4, 5, 7, 9, 11
N_WIN = CH_GATE
N_STREAM = N_WIN + 12 + 4
SCALE = HD ** -0.5


def build(nc, a, debug=None):
    names = set()

    with ExitStack() as ctx:
        ctx.enter_context(nc.allow_non_contiguous_dma(reason="small strided loads"))
        base = (nc.sbuf_base + 63) // 64 * 64

        def at(name, shape, off, dt=F32):
            assert name not in names and off % 32 == 0
            names.add(name)
            return nc.alloc_sbuf_tensor_at(name, shape, dt, offset=base + off)

        K = 1024
        x_T = at("x_T", [P, KD, TOK], 0)
        h_hi = at("h_hi", [P, KD, TOK], 20 * K, F32R)
        h_lo = at("h_lo", [P, KD, TOK], 40 * K, F32R)
        o = 60 * K
        ident = at("ident", [P, P], o)
        ones = at("ones", [P, P], o + 512)
        cond_T = at("cond_T", [P, KD, 2], o + 1024)
        mod_T = at("mod_T", [P, 48, 2], o + 1088)
        gain_T = at("gain_T", [P, 16], o + 1472)
        mul1 = at("mul1", [P, KD, 2], o + 1536)
        mul2 = at("mul2", [P, KD, 2], o + 1600)
        fin_gain = at("fin_gain", [P, KD], o + 1664)
        qk_gain = at("qk_gain", [P, 2, HD], o + 1696)
        sub_gain = at("sub_gain", [P, 1], o + 2208)
        lam_c = at("lam_c", [P, 2], o + 2240)
        neg_lam = at("neg_lam", [P, 1], o + 2272)
        wr_hi = at("wr_hi", [P, KD, NE], o + 2304, F32R)
        wr_lo = at("wr_lo", [P, KD, NE], o + 2816, F32R)
        bias_bc = at("bias_bc", [P, NE], o + 3328)
        tie = at("tie", [P, 4, 4], o + 3392)
        small = at("small_stats", [P, 4, 8], o + 3456)
        od_ss_row = at("od_ss_and_row_sum", [P, TT * DH + 2], o + 3584)
        od_ss, row_sum = od_ss_row[:, 0:TT * DH], od_ss_row[:, TT * DH:TT * DH + 2]
        od_r = at("od_r", [P, TT * DH], o + 3680)
        Z = o + 3776
        Z = (Z + 63) // 64 * 64
        LIMIT = nc.sbuf_usable_end - base

        psum = ctx.enter_context(nc.psum_tensor("psum", [P, 8, 512], F32))

        def pair(n):
            return psum[:, 2 * (n % 4):2 * (n % 4) + 2, :]

        def flat(n):
            return pair(n).rearrange("p a b -> p (a b)")

        sems = []

        def sem(name):
            s = ctx.enter_context(nc.semaphore(name))
            sems.append(s)
            return s

        comb_dram = nc.dram_tensor("comb_dram", (NE, TOK), F32, kind="Internal").ap()

        s_small = sem("small_loaded")
        s_store = sem("stores_done")
        n_t, n_h, n_hi, n_lo = (sem(x) for x in ("norm_scaled", "norm_h", "norm_hi", "norm_lo"))

        def clear():
            ids = [s.num for s in sems]
            nc.all_engine_barrier(sems_to_clear=range(min(ids), max(ids) + 1))

        n1 = [sem(f"norm1_{x}") for x in ("squares", "summed", "var", "std", "rstd")]
        n2 = [sem(f"norm2_{x}") for x in ("squares", "summed", "var", "std", "rstd")]
        nf = [sem(f"final_norm_{x}") for x in ("squares", "summed", "var", "std", "rstd")]

        def square(act, st, sq, kc):
            if kc >= 2:
                act.wait_ge(st[1], kc - 1)
            act.activation(sq[:, kc % 2, :], x_T[:, kc, :], ACT.Square).then_inc(st[0], 1)

        def sum_squares(pe, st, sq, kc):
            pe.wait_ge(st[0], kc + 1)
            for hf in range(2):
                mm = pe.matmul(pair(3)[:, hf, 0:HALF], ones[:, :], sq[:, kc % 2, hf * HALF:(hf + 1) * HALF],
                               start=(kc == 0), stop=(kc == KD - 1))
            mm.then_inc(st[1], 1)

        def root(act, st, var):
            act.wait_ge(st[2], 1)
            act.activation(var[:, :], var[:, :], ACT.Sqrt).then_inc(st[3], 1)

        def rstd_of(dve, st, var, rstd):
            dve.wait_ge(st[1], KD)
            dve.tensor_scalar(var[:, :].rearrange("p (a b) -> p a b", a=2), pair(3)[:, :, 0:HALF],
                              1.0 / D, EPS, ALU.mult, ALU.add).then_inc(st[2], 1)
            dve.wait_ge(st[3], 1)
            dve.reciprocal(rstd[:, :], var[:, :]).then_inc(st[4], 1)

        def modulate_act(act, h, mul, shift, kc):
            act.wait_ge(n_t, kc + 1)
            for s, (c0, c1) in enumerate(((0, N_PROMPT), (N_PROMPT, TOK))):
                act.activation(h[:, kc % NH, c0:c1], h[:, kc % NH, c0:c1], ACT.Identity,
                               bias=shift[:, kc, s:s + 1], scale=mul[:, kc, s:s + 1]).then_inc(n_h, 1)

        def modulate_dve(dve, h, rstd):
            for kc in range(KD + 1):
                if kc < KD:
                    if kc >= NH:
                        dve.wait_ge(n_lo, kc - NH + 1)
                    dve.tensor_tensor(h[:, kc % NH, :], x_T[:, kc, :], rstd[:, :], ALU.mult).then_inc(n_t, 1)
                if kc >= 1:
                    dve.wait_ge(n_h, 2 * kc)
                    dve.tensor_copy(h_hi[:, kc - 1, :], h[:, (kc - 1) % NH, :]).then_inc(n_hi, 1)

        def modulate_pool(pool, h, kc):
            pool.wait_ge(n_hi, kc + 1)
            pool.tensor_tensor(h_lo[:, kc, :], h[:, kc % NH, :], h_hi[:, kc, :].bitcast(F32),
                               ALU.subtract).then_inc(n_lo, 1)

        def mm_split(pe, out, st_hi, st_lo, mv_hi, mv_lo, start, stop):
            for n, (st, mv) in enumerate(((st_hi, mv_hi), (st_hi, mv_lo), (st_lo, mv_hi))):
                for q, dst in enumerate(out):
                    mm = pe.matmul(dst, st, mv[q], start=start and n == 0, stop=stop and n == 2)
            return mm

        def add_gated(dve, f, src, gate, done):
            parts = ((0, 0, 0, P), (1, 0, P, HALF), (1, 1, 0, HALF))
            for s, hf, c0, c1 in parts:
                xs = x_T[:, f, hf * HALF + c0:hf * HALF + c1]
                ins = dve.scalar_tensor_tensor(out=xs, in0=src[:, hf, c0:c1], scalar=gate[:, f, s:s + 1], in1=xs,
                                               op0=ALU.mult, op1=ALU.add)
            ins.then_inc(done, 1)

        s_xl, s_xt, s_xe, s_c1, s_c2, s_c3, s_c4, s_w1, s_w2 = (sem(x) for x in (
            "x_loaded", "x_turned", "x_evacuated", "cond_sigmoid", "cond_silu", "cond_turned", "cond_kept",
            "router_hi", "router_lo"))
        x_tok = at("x_tok", [P, TT, D], Z)
        cond_r = at("cond_r", [2, D], Z + 20 * K)
        cond_s = at("cond_s", [2, D], Z + 24 * K)
        cond_u = at("cond_u", [2, D], Z + 28 * K)
        wr_raw = at("wr_raw", [P, KD, NE], Z + 32 * K)
        fg_raw = at("fg_raw", [KD, P], Z + 33 * K)
        N_SMALL0 = 9
        with nc.Block() as block:
            @block.sync
            def _(sp):
                sp.dma_start(ident[:, :], a["c_ident"]).then_inc(s_small, 16)
                sp.dma_start(ones[:, :], a["c_ones"]).then_inc(s_small, 16)
                sp.dma_start(x_tok[:, 0, :], a["x_prompt"][0]).then_inc(s_xl, 16)
                sp.dma_start(x_tok[:, 1:TT, :], a["x_sample"][0].rearrange("(t p) d -> p t d", p=P)).then_inc(s_xl, 16)
                sp.dma_start(cond_r[0:1, :], a["c_ctx"].rearrange("(a n) -> a n", a=1)).then_inc(s_small, 16)
                sp.dma_start(cond_r[1:2, :], a["c"]).then_inc(s_small, 16)
                sp.dma_start(wr_raw[:, :, :], a["w_router"].rearrange("(k p) e -> p k e", p=P)).then_inc(s_small, 16)
                sp.dma_start(fg_raw[:, :], a["final_norm_g"].rearrange("(k p) -> k p", p=P)).then_inc(s_small, 16)
                sp.dma_start(bias_bc[:, :], a["router_bias"].partition_broadcast(P)).then_inc(s_small, 16)
                sp.dma_start(tie[:, :, :], a["c_tie"].partition_broadcast(P)).then_inc(s_small, 16)
                sp.dma_start(row_sum[:, :], a["c_row_sum"]).then_inc(s_small, 16)
                sp.wait_ge(s_small, 16 * N_SMALL0)

            @block.tensor
            def _(pe):
                pe.wait_ge(s_small, 16 * N_SMALL0)
                pe.wait_ge(s_xl, 32)
                for kc in range(KD):
                    if kc >= 3:
                        pe.wait_ge(s_xe, kc - 2)
                    for t in range(TT):
                        mm = pe.transpose(flat(kc % 3)[:, t * P:(t + 1) * P], x_tok[:, t, kc * P:(kc + 1) * P],
                                          ident[:, :])
                    mm.then_inc(s_xt, 1)
                pe.wait_ge(s_c2, 1)
                for kc in range(KD):
                    pe.transpose(flat(3)[:, 2 * kc:2 * kc + 2], cond_u[:, kc * P:(kc + 1) * P], ident[0:2, 0:2])
                pe.transpose(flat(3)[:, 512:512 + KD], fg_raw[:, :], ident[0:KD, 0:KD]).then_inc(s_c3, 1)

            @block.scalar
            def _(act):
                act.wait_ge(s_small, 16 * N_SMALL0)
                act.activation(cond_s[:, :], cond_r[:, :], ACT.Sigmoid).then_inc(s_c1, 1)
                act.activation(wr_hi[:, :, :], wr_raw[:, :, :], ACT.Copy).then_inc(s_w1, 1)

            @block.vector
            def _(dve):
                dve.wait_ge(s_c1, 1)
                dve.tensor_tensor(cond_u[:, :], cond_r[:, :], cond_s[:, :], ALU.mult).then_inc(s_c2, 1)
                dve.wait_ge(s_w1, 1)
                dve.tensor_tensor(wr_lo[:, :, :], wr_raw[:, :, :], wr_hi[:, :, :].bitcast(F32),
                                  ALU.subtract).then_inc(s_w2, 1)
                for kc in range(KD):
                    dve.wait_ge(s_xt, kc + 1)
                    dve.tensor_copy(x_T[:, kc, :], flat(kc % 3)[:, 0:TOK]).then_inc(s_xe, 1)
                dve.wait_ge(s_c3, 1)
                dve.tensor_copy(cond_T[:, :, :], flat(3)[:, 0:2 * KD].rearrange("p (k s) -> p k s", s=2)).then_inc(s_c4, 1)
                dve.tensor_copy(fin_gain[:, :], flat(3)[:, 512:512 + KD]).then_inc(s_c4, 1)
        clear()

        MC = 2 * D // 512
        MC2 = 4 * D // WC
        MB2 = 2 * D // P
        wm = [at(f"wm{i}", [P, KD, 512], Z + 56 * K + 16 * K * i) for i in range(3)]
        mod_rows = at("mod_rows", [P, 2, 512], Z + 104 * K)
        T = Z + 139 * K
        row_in = at("row_in", [64, P], T)
        lam_in = at("lam_in", [P, 2, 2, HD], T + K // 2)
        lam_pr = at("lam_pr", [P, 2, HD], T + 3 * K // 2)
        lam_s = at("lam_s", [P, 2], T + 2 * K)
        lam_e = at("lam_e", [P, 2], T + 2 * K + 32)
        lam_d = at("lam_d", [P, 1], T + 2 * K + 64)
        sub_raw = at("sub_raw", [P, 1], T + 2 * K + 96)
        bias_T = at("bias_T", [P, 48], T + 2 * K + 160)
        mod_rows2 = at("mod_rows2", [P, 2, WC], Z + 54 * K)
        m2_ld = [sem(f"wmod_rest_loaded{i}") for i in range(2)]
        m2_0, m2_mm, m2_ev, m2_tr, m2_cp = (sem(x) for x in (
            "mod_rest_cleared", "mod_rest_product", "mod_rest_evacuated", "mod_rest_turned", "mod_rest_kept"))
        m_ld = [sem(f"wmod_loaded{i}") for i in range(3)]
        m_0, m_mm, m_ev, m_tr, m_cp, m_done, m_l = (sem(x) for x in (
            "mod_rows_cleared", "mod_product", "mod_evacuated", "mod_turned", "mod_kept", "mod_done", "lambda_step"))

        M = Z
        raw = [at(f"raw{i}", [P, KD, WC], M + 8 * K * i) for i in range(2)]
        whi = [at(f"whi{i}", [P, KD, WC], M + 16 * K + 8 * K * i, F32R) for i in range(2)]
        wlo = [at(f"wlo{i}", [P, KD, WC], M + 32 * K + 8 * K * i, F32R) for i in range(2)]
        M += 48 * K
        pw = [at(f"pw{i}", [P, 4, WC], M + 4 * K * i) for i in range(2)]
        M += 8 * K
        y_T = at("y_T", [P, FG, TOK], M)
        q_T = at("q_T", [P, 8, TOK], M + 10 * K)
        k_T = at("k_T", [P, 6, KEYS + N_PROMPT], M + 30 * K)
        v_tok = at("v_tok", [P, 6, 640], M + 48 * K)
        R = M + 63 * K
        assert R + 25 * K <= LIMIT, (R + 25 * K, LIMIT)
        u_T = at("u_T", [P, FG, TOK], M + 10 * K)
        dft_tab = at("dft_tab", [P, 2, 4, 512], M + 20 * K)
        dft_ch = at("dft_ch", [P, 2 * P], M + 36 * K)
        dft_pr = at("dft_pr", [P, 2, P], M + 37 * K)
        ab = at("ab", [P, 2, TT, 2 * P], M + 38 * K)
        sq_mix = at("sq_mix", [P, 2, TOK], R)
        var_mix = at("var_mix", [P, TOK], R + 5 * K)
        rstd_mix = at("rstd_mix", [P, TOK], R + 7680)
        h_mix = at("h_mix", [P, NH, TOK], R)
        z_s = at("z_s", [P, 4, WC], R)
        z_r = at("z_r", [P, 4, WC], R + 4 * K)
        z_t = at("z_t", [P, WC], R + 8 * K)
        z_q = at("z_q", [P, WC], R + 9 * K)
        z_ss = at("z_ss", [P, 4], R + 10 * K)
        z_v = at("z_v", [P, 4], R + 10 * K + 32)
        z_d = at("z_d", [P, 4], R + 10 * K + 64)
        z_i = at("z_i", [P, 4], R + 10 * K + 96)
        k_cache = at("k_cache", [P, 6, P], R + 15 * K)
        rope = at("rope", [P, 2, 4, HD], R + 18 * K)
        k_out_g = at("k_out_g", [P, P], R + 20 * K)
        k_out_d = at("k_out_d", [P, 512], R + 20 * K + 512)
        prob = at("prob", [P, 4, KEYS], R)
        prob_T = at("prob_T", [P, 2, 5, P], R + 10 * K)
        od = at("od", [P, TT, DH, P], R + 15 * K)
        mg_hi = at("mg_hi", [P, KD, TOK], M + 30 * K, F32R)
        mg_lo = at("mg_lo", [P, KD, TOK], M + 50 * K, F32R)
        sig_m = at("sig_m", [P, 2, TOK], M + 70 * K)
        mg = at("mg", [P, 2, TOK], M + 75 * K)
        mg_t = at("mg_t", [P, TOK], M + 80 * K)
        rstd2 = at("rstd2", [P, TOK], M + 70 * K)
        var2 = at("var2", [P, TOK], M + 72 * K + K // 2)
        sq2 = at("sq2", [P, 2, TOK], M + 75 * K)
        q_pad = at("q_pad", [P, 4, P], Z + 52 * K)

        w_ld = [sem(f"weights_loaded{i}") for i in range(2)]
        w_hi, w_lo = sem("weights_hi"), sem("weights_lo")
        p_ld = [sem(f"out_weights_loaded{i}") for i in range(2)]
        s_full, s_free = sem("psum_full"), sem("psum_free")
        s_z, s_rope, s_vs, s_va, s_kc, s_cv = (sem(x) for x in (
            "rows_used", "rope_done", "row_square", "row_sqrt", "k_cache_loaded", "v_cache_loaded"))
        s_r = sem("rope_step")
        t_s, t_max, t_exp, t_p, t_tr, t_pt, t_pv, t_o, t_l = (sem(x) for x in (
            "scores_ready", "max_ready", "exp_done", "probs_ready", "probs_turned", "probs_T_kept",
            "pv_ready", "pv_kept", "sum_inverted"))
        t_q0, t_q = sem("q_pad_cleared"), sem("q_padded")
        d_sq, d_1, d_2, d_3, d_t, d_k = (sem(x) for x in (
            "subln_squares", "subln_var", "subln_sqrt", "subln_scaled", "subln_turned", "subln_kept"))
        g_full, g_sig, g_pfull, g_pfree, g_acc, g_hi, g_lo = (sem(x) for x in (
            "gate_ready", "gate_sigmoid", "branch_ready", "branch_used", "merge_step", "merged_hi", "merged_lo"))
        o_full, o_add = sem("w_out_ready"), sem("residual_added")

        units = [("u", g) for g in range(FG)]
        units += [("ab", 0, 0), ("ab", 0, 1), ("ab", 1, 0), ("ab", 1, 1)]
        for g in range(FG):
            units.append(("y", g))
            if g + 2 < FG:
                units += [("ab", g + 2, 0), ("ab", g + 2, 1)]
        units.append(("kcache",))
        rows = [(c, t) for c in range(CH_QG, N_WIN) for t in range(TT)]
        turned = [r for r in rows if r[0] < CH_VD]
        LAG = 3
        for i in range(len(rows) + LAG):
            if i < len(rows):
                units.append(("z",) + rows[i])
            if LAG <= i < LAG + len(turned):
                units.append(("x",) + turned[i - LAG])
        unit_no = {u: n for n, u in enumerate(units)}
        n_x = {r: n for n, r in enumerate(turned)}

        def is_gqa(c):
            return c < CH_QD

        def key_tile(t):
            return 5 if t == 0 else t

        att = [("g", 2 * hp + b, t) for hp in range(QH // 2) for t in range(TT) for b in range(2)]
        att += [("d", h, t) for h in range(DH) for t in range(TT)]
        maps, first_map = [], []
        for u in att:
            first_map.append(len(maps))
            maps += [u + (m,) for m in range(1 if u[0] == "g" else 2)]
        map_end = first_map[1:] + [len(maps)]

        def q_slice(kind, h, t, m):
            if kind == "g":
                r = HD * (h % 2)
                return q_T[r:r + HD, h // 2, t * P:(t + 1) * P]
            return q_T[HD * m:HD * m + HD, 4 + h, t * P:(t + 1) * P]

        def k_slice(kind, h, c0, c1):
            return k_T[:, h // (QH // KVH) if kind == "g" else 2 + h, c0:c1]

        MOD_END = 3 * MC2 + 1

        def mod_step(i):
            return i // 3 if i % 3 == 1 and i < MOD_END else None

        def key_tiles(t):
            return [5] if t == 0 else [0, 1, 2, 3, 4]

        def scores_view(n, t):
            return flat(n % 2)[:, 0:P] if t == 0 else pair(n % 2)[:, :, 0:HALF]

        def prob_view(n, t):
            w = P if t == 0 else KEYS
            v = prob[:, n % 4, 0:w]
            return v if t == 0 else v.rearrange("p (a b) -> p a b", a=2)

        E0 = Z
        ex = {}
        for n, r in enumerate("gud"):
            shape = [P, 2, D] if r == "d" else [P, KD, DE]
            ex[r] = (at(f"xw_raw_{r}", shape, E0 + 24 * K * n), at(f"xw_hi_{r}", shape, E0 + 24 * K * n + 8 * K, F32R),
                     at(f"xw_lo_{r}", shape, E0 + 24 * K * n + 16 * K, F32R))
        E0 += 72 * K
        y_acc = at("y_acc", [P, KD, TOK], E0)
        act_f = at("act_f", [P, 2, TOK], E0 + 20 * K)
        act_hi = at("act_hi", [P, 2, TOK], E0 + 25 * K, F32R)
        act_lo = at("act_lo", [P, 2, TOK], E0 + 30 * K, F32R)
        sig_x = at("sig_x", [P, 2, TOK], E0 + 35 * K)
        cb = at("cb", [P, 2, TOK], E0 + 40 * K)
        h_moe = at("h_moe", [P, NH, TOK], E0 + 45 * K)
        RT = E0 + 60 * K
        logits = at("logits", [NE, TOK], RT)
        comb_T = at("comb_T", [NE, TOK], RT)
        rt_n = [0]

        def rt(name, n):
            rt_n[0] += 1
            return at(name, [P, n], RT + 2560 + 320 * (rt_n[0] - 1))
        sc = rt("rt_scores", TT * NE)
        sel = rt("rt_select", TT * NE)
        rank = rt("rt_rank", TT * NE)
        top2 = rt("rt_top2", TT * NE)
        tmp16 = rt("rt_tmp", TT * NE)
        grp = rt("rt_group", TT * NG)
        grank = rt("rt_grank", TT * NG)
        gbest = rt("rt_gbest", TT * NG)
        wsum = rt("rt_wsum", TT)
        wrec = rt("rt_wrec", TT)
        comb = rt("rt_comb", TT * NE)
        cmp_gt = at("rt_gt", [P, TT * NG * 16], RT + 2560 + 320 * 11)
        cmp_eq = at("rt_eq", [P, TT * NG * 16], RT + 2560 + 320 * 11 + 1280)
        assert RT + 2560 + 320 * 11 + 2560 <= LIMIT
        x_ld = {r: sem(f"expert_{r}_loaded") for r in "gud"}
        x_hi = {r: sem(f"expert_{r}_hi") for r in "gud"}
        x_lo = {r: sem(f"expert_{r}_lo") for r in "gud"}
        r_lg, r_sg, r_st, r_ct, r_ce, r_cs = (sem(x) for x in (
            "router_logits", "router_scores", "routing_step", "combine_turned", "combine_kept", "combine_stored"))
        c_ld = sem("combine_loaded")
        x_full, x_free, x_sig, x_ahi, x_alo, x_sg, x_y0 = (sem(x) for x in (
            "expert_psum_full", "expert_psum_free", "expert_sigmoid", "expert_act_hi",
            "expert_act_lo", "expert_gated", "y_cleared"))
        r_lk, r_lt = sem("logits_kept"), sem("logits_turned")
        x_step = sem("moe_residual")
        ROUTE_STEPS = 20

        with nc.Fori(0, DEPTH) as layer:
            shift1, gate1 = mod_T[:, 0:8, :], mod_T[:, 16:24, :]
            shift2, gate2 = mod_T[:, 24:32, :], mod_T[:, 40:48, :]
            with nc.Block() as block:
                @block.sync
                def _(sp):
                    w_mod = a["w_mod"][layer].rearrange("(k p) n -> p k n", p=P)
                    w_in = a["w_in"][layer].rearrange("(k p) n -> p k n", p=P)
                    w_out = a["w_out"][layer].rearrange("(k p) n -> p k n", p=P)
                    w_br = [a[n][layer].rearrange("(k p) n -> p k n", p=P) for n in ("w_fourier", "w_gqa_o", "w_diff_o")]

                    def stream(i):
                        if i >= 2:
                            sp.wait_ge(w_lo, i - 1)
                        if i < N_WIN:
                            src = w_in[:, :, i * WC:(i + 1) * WC]
                        elif i < N_WIN + 12:
                            m, b = divmod(i - N_WIN, 3)
                            c0 = IN_COLS + b * D + m * WC
                            src = w_in[:, :, c0:c0 + WC]
                        else:
                            m = i - N_WIN - 12
                            src = w_out[:, :, m * WC:(m + 1) * WC]
                        sp.dma_start(raw[i % 2][:, :, :], src).then_inc(w_ld[i % 2], 16)

                    sp.dma_start(row_in[0:8, :], a["norm1_g"][layer].rearrange("(k p) -> k p", p=P)).then_inc(s_small, 16)
                    sp.dma_start(row_in[8:16, :], a["norm2_g"][layer].rearrange("(k p) -> k p", p=P)).then_inc(s_small, 16)
                    sp.dma_start(row_in[16:64, :], a["b_mod"][layer].rearrange("(k p) -> k p", p=P)).then_inc(s_small, 16)
                    sp.dma_start(qk_gain[:, 0, :], a["gqa_q_norm"][layer].partition_broadcast(P)).then_inc(s_small, 16)
                    sp.dma_start(qk_gain[:, 1, :], a["gqa_k_norm"][layer].partition_broadcast(P)).then_inc(s_small, 16)
                    sp.dma_start(sub_raw[:, :], a["diff_subln_g"][layer].rearrange("(p a) -> p a", a=1)).then_inc(s_small, 16)
                    sp.dma_start(lam_c[:, :], a["c_lambda"][layer].partition_broadcast(P)).then_inc(s_small, 16)
                    sp.dma_start(lam_in[:, :, :, :].rearrange("p a b d -> p (a b) d"),
                                 a["diff_lambda"][layer].partition_broadcast(P)).then_inc(s_small, 16)
                    for j in range(MC):
                        if j >= 3:
                            sp.wait_ge(m_mm, j - 2)
                        if j == MC - 1:
                            stream(0)
                        sp.dma_start(wm[j % 3][:, :, :], w_mod[:, :, j * 512:(j + 1) * 512]).then_inc(m_ld[j % 3], 16)
                    stream(1)
                    sp.wait_ge(m_tr, MC)
                    sp.dma_start(dft_tab[:, :, :, :], a["c_dft"]).then_inc(s_small, 16)
                    sp.dma_start(dft_ch[:, :], a["c_dft_ch"]).then_inc(s_small, 16)
                    sp.dma_start(dft_pr[:, :, :], a["c_dft_pr"]).then_inc(s_small, 16)
                    sp.dma_start(rope[:, :, :, :], a["c_rope"]).then_inc(s_small, 16)
                    kg = a["cache_gqa_k"][0, layer]
                    for dup in range(2):
                        sp.dma_start(k_cache[:, 0:2, dup * HD:(dup + 1) * HD], kg).then_inc(s_kc, 16)
                    sp.dma_start(k_cache[:, 2:6, :], a["cache_diff_k"][0, layer].rearrange("n h m d -> n h (m d)")).then_inc(s_kc, 16)
                    sp.dma_start(v_tok[:, 0, 0:P], a["cache_gqa_v"][0, layer].rearrange("n h d -> n (h d)")).then_inc(s_cv, 16)
                    sp.dma_start(v_tok[:, 0, P:640], a["cache_diff_v"][0, layer].rearrange("n h d -> n (h d)")).then_inc(s_cv, 16)
                    for i in range(2, N_WIN + 2):
                        stream(i)
                    sp.wait_ge(s_rope, n_x[(CH_KVG, 0)] + 1)
                    sp.dma_start(a["new_gqa_k"][0, layer].rearrange("n h d -> n (h d)"), k_out_g[:, :]).then_inc(s_store, 16)
                    sp.wait_ge(s_free, unit_no[("z", CH_VD + 1, 0)] + 1)
                    sp.dma_start(a["new_diff_k"][0, layer].rearrange("n h m d -> n (h m d)"), k_out_d[:, :]).then_inc(s_store, 16)
                    sp.dma_start(a["new_gqa_v"][0, layer].rearrange("n h d -> n (h d)"), v_tok[:, 5, 0:P]).then_inc(s_store, 16)
                    sp.dma_start(a["new_diff_v"][0, layer].rearrange("n h d -> n (h d)"), v_tok[:, 5, P:640]).then_inc(s_store, 16)
                    for k in range(MC2):
                        if k < 2:
                            sp.wait_ge(w_lo, N_WIN + 1 + k)
                        else:
                            sp.wait_ge(m2_mm, k - 1)
                        c0 = 2 * D + k * WC
                        sp.dma_start(raw[(N_WIN + k) % 2][:, :, :], w_mod[:, :, c0:c0 + WC]).then_inc(m2_ld[k % 2], 16)
                    sp.wait_ge(m2_mm, MC2)
                    stream(N_WIN + 2)
                    stream(N_WIN + 3)
                    for n in range(12):
                        m, b = divmod(n, 3)
                        if n == 1:
                            sp.wait_ge(t_s, len(maps))
                        if n >= 2:
                            sp.wait_ge(g_pfull, 2 * (n - 1))
                        sp.dma_start(pw[n % 2][:, :, :], w_br[b][:, :, m * WC:(m + 1) * WC]).then_inc(p_ld[n % 2], 16)
                        if n >= 1:
                            stream(N_WIN + 3 + n)
                    stream(N_STREAM - 1)
                    sp.wait_ge(s_store, 16 * 4)

                @block.gpsimd
                def _(pool):
                    pool.memset(mod_rows[:, :, :], 0.0).then_inc(m_0, 1)
                    pool.wait_ge(m_0, 1)
                    pool.memset(q_pad[HD:P, 0:4:2, :], 0.0).then_inc(t_q0, 1)
                    pool.wait_ge(t_q0, 1)
                    pool.memset(mod_rows2[:, :, :], 0.0).then_inc(m2_0, 1)
                    pool.wait_ge(m2_0, 1)
                    pool.memset(q_pad[0:HD, 1:4:2, :], 0.0).then_inc(t_q0, 1)

                    def lo(i):
                        pool.wait_ge(w_hi, i + 1)
                        pool.tensor_tensor(wlo[i % 2][:, :, :], raw[i % 2][:, :, :], whi[i % 2][:, :, :].bitcast(F32),
                                           ALU.subtract).then_inc(w_lo, 1)
                    lo(0)
                    for kc in range(KD):
                        modulate_pool(pool, h_mix, kc)
                    lo(1)
                    for i in range(2, N_WIN + 1):
                        lo(i)
                    pool.wait_ge(t_q0, 2)
                    pool.wait_ge(w_lo, N_WIN + 1)
                    for n, (kind, h, t, m) in enumerate(maps):
                        if n == 0:
                            pool.wait_ge(s_free, unit_no[("x", CH_QG + 1, TT - 1)] + 1)
                        if n == QH * TT:
                            pool.wait_ge(s_free, unit_no[("x", CH_QD + 1, TT - 1)] + 1)
                        if n >= 1:
                            pool.wait_ge(t_q, n)
                        if n == 4:
                            lo(N_WIN + 1)
                            pool.wait_ge(w_lo, N_WIN + 2)
                        if n >= 4:
                            pool.wait_ge(t_s, n - 3)
                        r = HD * (n % 2)
                        pool.tensor_copy(q_pad[r:r + HD, n % 4, :], q_slice(kind, h, t, m)).then_inc(t_q, 1)
                    pool.wait_ge(t_q, len(maps))
                    for m in range(4):
                        for b in range(3):
                            if N_WIN + 3 * m + b + 2 < N_STREAM:
                                lo(N_WIN + 3 * m + b + 2)
                        for fc in range(2):
                            pool.wait_ge(g_hi, 2 * m + fc + 1)
                            pool.tensor_tensor(mg_lo[:, 2 * m + fc, :], mg[:, fc, :], mg_hi[:, 2 * m + fc, :].bitcast(F32),
                                               ALU.subtract).then_inc(g_lo, 1)
                    for i in range(N_WIN + 14, N_STREAM):
                        lo(i)

                @block.scalar
                def _(act):
                    def hi(i):
                        act.wait_ge(w_ld[i % 2], 16 * (i // 2 + 1))
                        act.activation(whi[i % 2][:, :, :], raw[i % 2][:, :, :], ACT.Copy).then_inc(w_hi, 1)

                    for kc in range(KD):
                        square(act, n1, sq_mix, kc)
                    root(act, n1, var_mix)
                    act.wait_ge(m_l, 2)
                    act.activation(lam_e[:, :], lam_s[:, :], ACT.Exp).then_inc(m_l, 1)
                    act.wait_ge(m_0, 1)
                    for j in range(MC):
                        if j == MC - 1:
                            hi(0)
                        act.wait_ge(m_mm, j + 1)
                        if j >= 2:
                            act.wait_ge(m_tr, j - 1)
                        for q in range(4):
                            act.activation(mod_rows[32 * q:32 * q + 2, j % 2, :], psum[32 * q:32 * q + 2, j % 2, :],
                                           ACT.Copy).then_inc(m_ev, 1)
                    for kc in range(2):
                        modulate_act(act, h_mix, mul1, shift1, kc)
                    hi(1)
                    for kc in range(2, KD):
                        modulate_act(act, h_mix, mul1, shift1, kc)
                    n_sqrt = 0
                    for n, u in enumerate(units):
                        act.wait_ge(s_full, n + 1)
                        if u[0] == "u":
                            act.activation(u_T[:, u[1], :].rearrange("p (a b) -> p a b", a=2), pair(n)[:, :, 0:HALF],
                                           ACT.Copy).then_inc(s_free, 1)
                            if u[1] % 2 == 1:
                                hi(u[1] // 2 + 2)
                        elif u[0] == "ab":
                            g, part = u[1:]
                            t0, t1 = ((0, 4), (4, 5))[part]
                            act.activation(ab[:, g % 2, t0:t1, :].rearrange("p t c -> p (t c)"),
                                           flat(n)[:, 0:(t1 - t0) * 2 * P], ACT.Copy).then_inc(s_free, 1)
                        elif u[0] == "y":
                            act.activation(y_T[:, u[1], 0:P], pair(n)[:, 0, 0:P], ACT.Copy)
                            act.activation(y_T[:, u[1], P:TOK], pair(n)[:, 1, :], ACT.Copy).then_inc(s_free, 1)
                        elif u[0] == "kcache":
                            act.activation(k_T[:, :, 0:P], flat(n)[:, 0:6 * P].rearrange("p (c k) -> p c k", c=6),
                                           ACT.Copy).then_inc(s_free, 1)
                        elif u[0] == "z":
                            c, t = u[1:]
                            if c < CH_VD:
                                i = n_x[(c, t)]
                                if i >= 4:
                                    act.wait_ge(s_rope, i - 3)
                            if c == CH_KVG:
                                act.activation(v_tok[:, key_tile(t), 0:P], flat(n)[:, P:2 * P], ACT.Copy)
                                act.activation(z_s[:, i % 4, 0:P], flat(n)[:, 0:P], ACT.Copy).then_inc(s_free, 1)
                            elif c >= CH_VD:
                                c0 = P + (c - CH_VD) * WC
                                act.activation(v_tok[:, key_tile(t), c0:c0 + WC], flat(n)[:, 0:WC], ACT.Copy).then_inc(s_free, 1)
                            else:
                                if c in (CH_KD, CH_KD + 1) and t == 0:
                                    c0 = (c - CH_KD) * WC
                                    act.activation(k_out_d[:, c0:c0 + WC], flat(n)[:, 0:WC], ACT.Copy)
                                act.activation(z_s[:, i % 4, :], flat(n)[:, 0:WC], ACT.Copy).then_inc(s_free, 1)
                            if c < CH_QD:
                                w = P if c == CH_KVG else WC
                                if n_sqrt:
                                    act.wait_ge(s_vs, 3 * n_sqrt)
                                act.wait_ge(s_free, n + 1)
                                act.activation(z_q[:, 0:w], z_s[:, i % 4, 0:w], ACT.Square).then_inc(s_vs, 1)
                                act.wait_ge(s_vs, 3 * n_sqrt + 3)
                                act.activation(z_d[:, 0:w // HD], z_v[:, 0:w // HD], ACT.Sqrt).then_inc(s_va, 1)
                                n_sqrt += 1
                            if t == TT - 1 and c + 2 <= CH_GATE + 1:
                                hi(c + 2)
                        else:
                            c, t = u[1:]
                            kt = key_tile(t)
                            src = flat(n)[:, 0:WC].rearrange("p (c k) -> p c k", c=2)
                            if c in (CH_QG, CH_QG + 1, CH_QD, CH_QD + 1):
                                q0 = 2 * (c - CH_QG) if c < CH_QD else 4 + 2 * (c - CH_QD)
                                act.activation(q_T[:, q0:q0 + 2, t * P:(t + 1) * P], src, ACT.Copy,
                                               scale=SCALE).then_inc(s_free, 1)
                            else:
                                k0 = 0 if c == CH_KVG else 2 + 2 * (c - CH_KD)
                                act.activation(k_T[:, k0:k0 + 2, kt * P:(kt + 1) * P], src, ACT.Copy).then_inc(s_free, 1)

                    def exps(i):
                        for n in range(first_map[i], map_end[i]):
                            t = maps[n][2]
                            act.wait_ge(t_max, n + 1)
                            if n >= 4:
                                act.wait_ge(t_tr, max(j for j in range(len(att)) if first_map[j] <= n - 4) + 1)
                            act.activation(prob_view(n, t), scores_view(n, t), ACT.Exp, bias=small[:, n % 4, 0:1],
                                           accum_out=small[:, n % 4, 1:2]).then_inc(t_exp, 1)

                    def keep_T(i):
                        w = P * len(key_tiles(att[i][2]))
                        act.wait_ge(t_tr, i + 1)
                        if i >= 2:
                            act.wait_ge(t_pv, i - 1)
                        act.activation(prob_T[:, i % 2, :, :].rearrange("p t q -> p (t q)")[:, 0:w], flat(2)[:, 0:w],
                                       ACT.Copy).then_inc(t_pt, 1)
                        k = mod_step(i)
                        if k is not None:
                            if k == 0:
                                act.wait_ge(m2_0, 1)
                            if k >= 2:
                                act.wait_ge(m2_tr, k - 1)
                            for q in range(4):
                                act.activation(mod_rows2[32 * q:32 * q + 2, k % 2, :], psum[32 * q:32 * q + 2, 5, 256:512],
                                               ACT.Copy).then_inc(m2_ev, 1)

                    for i in range(len(att) + 3):
                        if i < len(att):
                            exps(i)
                        if 2 <= i < len(att) + 2:
                            keep_T(i - 2)
                    act.wait_ge(t_o, len(att))
                    for j in range(TT * DH):
                        t, h = divmod(j, DH)
                        if j >= 4:
                            act.wait_ge(d_sq, j - 3)
                        act.activation(prob[:, j % 4, 0:P], od[:, t, h, :], ACT.Square,
                                       accum_out=od_ss[:, j:j + 1]).then_inc(d_sq, 1)
                    act.wait_ge(d_1, 1)
                    act.activation(od_r[:, :], od_ss[:, :], ACT.Sqrt).then_inc(d_2, 1)
                    for m in range(4):
                        for b in range(3):
                            for fc in range(2):
                                g = 6 * m + 2 * b + fc
                                act.wait_ge(g_full, g + 1)
                                if g >= 2:
                                    act.wait_ge(g_pfree, g - 1)
                                act.activation(sig_m[:, g % 2, :].rearrange("p (a b) -> p a b", a=2),
                                               pair(g % 2)[:, :, 0:HALF], ACT.Sigmoid).then_inc(g_sig, 1)
                            if (m, b) == (0, 0):
                                for h in range(DH):
                                    act.wait_ge(d_t, h + 1)
                                    act.activation(q_T[:, 4 + h, :], flat(h % 2)[:, 0:TOK], ACT.Copy,
                                                   scale=sub_gain[:, 0:1]).then_inc(d_k, 1)
                            if N_WIN + 3 * m + b + 2 < N_STREAM:
                                hi(N_WIN + 3 * m + b + 2)
                        for fc in range(2):
                            act.wait_ge(g_acc, 4 * (m + 1))
                            act.activation(mg_hi[:, 2 * m + fc, :], mg[:, fc, :], ACT.Copy).then_inc(g_hi, 1)
                    for f in range(KD):
                        act.wait_ge(o_add, f + 1)
                        square(act, n2, sq2, f)
                        if f % 2 == 1 and N_WIN + 14 + f // 2 < N_STREAM:
                            hi(N_WIN + 14 + f // 2)
                    root(act, n2, var2)

                @block.vector
                def _(dve):
                    dve.wait_ge(s_small, 16 * 8)
                    dve.tensor_tensor(lam_pr[:, :, :], lam_in[:, :, 0, :], lam_in[:, :, 1, :], ALU.mult).then_inc(m_l, 1)
                    dve.wait_ge(m_l, 1)
                    dve.tensor_reduce(lam_s[:, :], lam_pr[:, :, :], AX.X, ALU.add).then_inc(m_l, 1)
                    dve.tensor_scalar(sub_gain[:, :], sub_raw[:, :], lam_c[:, 1:2], None, ALU.mult)
                    rstd_of(dve, n1, var_mix, rstd_mix)
                    dve.wait_ge(m_l, 3)
                    dve.tensor_tensor(lam_d[:, :], lam_e[:, 1:2], lam_e[:, 0:1], ALU.subtract).then_inc(m_l, 1)
                    dve.wait_ge(m_l, 4)
                    dve.tensor_tensor(neg_lam[:, :], lam_d[:, :], lam_c[:, 0:1], ALU.subtract).then_inc(m_l, 1)
                    dve.wait_ge(m_tr, 1)
                    dve.tensor_copy(gain_T[:, :], psum[:, 4, 0:16]).then_inc(m_cp, 1)
                    dve.tensor_copy(bias_T[:, :], psum[:, 4, 16:64]).then_inc(m_cp, 1)
                    dve.wait_ge(m_cp, 2)
                    dve.tensor_copy(mod_T[:, MB2:48, :], bias_T[:, MB2:48].unsqueeze(2).to_broadcast([P, 48 - MB2, 2])).then_inc(m_cp, 1)
                    dve.wait_ge(m_tr, MC)
                    dve.tensor_tensor(mod_T[:, 0:MB2, :], psum[:, 5, 0:2 * MB2].rearrange("p (c s) -> p c s", s=2),
                                      bias_T[:, 0:MB2].unsqueeze(2).to_broadcast([P, MB2, 2]), ALU.add).then_inc(m_cp, 1)
                    dve.wait_ge(m_cp, 4)

                    def scaled_gain(mul, col, g0):
                        return dve.scalar_tensor_tensor(
                            out=mul[:, :, :], in0=mod_T[:, col:col + 8, :], scalar=1.0,
                            in1=gain_T[:, g0:g0 + 8].unsqueeze(2).to_broadcast([P, KD, 2]), op0=ALU.add, op1=ALU.mult)

                    scaled_gain(mul1, 8, 0).then_inc(m_done, 1)
                    dve.wait_ge(n1[4], 1)
                    modulate_dve(dve, h_mix, rstd_mix)
                    dve.wait_ge(s_small, 16 * 12)
                    n_rope = [0]

                    def step(ins):
                        n_rope[0] += 1
                        ins.then_inc(s_r, 1)
                        dve.wait_ge(s_r, n_rope[0])

                    n_sqrt = 0
                    for i, (c, t) in enumerate(turned):
                        zn = unit_no[("z", c, t)]
                        w = P if c == CH_KVG else WC
                        nh = w // HD
                        zin = z_s[:, i % 4, 0:w]
                        heads = zin.rearrange("p (h d) -> p h d", d=HD)
                        dve.wait_ge(s_free, zn + 1)
                        if i >= 1:
                            dve.wait_ge(s_rope, i)
                        if i >= 4:
                            dve.wait_ge(s_full, unit_no[("x",) + turned[i - 4]] + 1)
                        if is_gqa(c):
                            dve.wait_ge(s_vs, 3 * n_sqrt + 1)
                            dve.tensor_reduce(z_ss[:, 0:nh], z_q[:, 0:w].rearrange("p (h d) -> p h d", d=HD),
                                              AX.X, ALU.add).then_inc(s_vs, 1)
                            dve.wait_ge(s_vs, 3 * n_sqrt + 2)
                            dve.tensor_scalar(z_v[:, 0:nh], z_ss[:, 0:nh], 1.0 / HD, EPS, ALU.mult, ALU.add).then_inc(s_vs, 1)
                            dve.wait_ge(s_va, n_sqrt + 1)
                            step(dve.reciprocal(z_i[:, 0:nh], z_d[:, 0:nh]))
                            step(dve.tensor_tensor(heads, heads, z_i[:, 0:nh].unsqueeze(2).to_broadcast([P, nh, HD]), ALU.mult))
                            gain = qk_gain[:, 1 if c == CH_KVG else 0, :].unsqueeze(1).to_broadcast([P, nh, HD])
                            step(dve.tensor_tensor(heads, heads, gain, ALU.mult))
                            n_sqrt += 1
                        if c == CH_KVG:
                            dst = z_r[:, i % 4, :].rearrange("p (h u d) -> p h u d", h=2, u=2)
                            outs = [dst[:, :, 0, :], dst[:, :, 1, :]]
                        else:
                            outs = [z_r[:, i % 4, :].rearrange("p (h d) -> p h d", d=HD)]
                        if t == 0:
                            if c == CH_KVG:
                                dve.tensor_copy(k_out_g[:, :], zin)
                                dve.tensor_copy(outs[1], heads)
                            dve.tensor_copy(outs[0], heads).then_inc(s_rope, 1)
                            continue
                        cos = rope[:, 0, t - 1, :].unsqueeze(1).to_broadcast([P, nh, HD])
                        halves = zin.rearrange("p (h a b d) -> p h a b d", a=2, b=2, d=16)
                        turned_h = z_t[:, 0:w].rearrange("p (h a b d) -> p h a b d", a=2, b=2, d=16)
                        sin = rope[:, 1, t - 1, :].rearrange("p (a b d) -> p a b d", a=2, b=2)
                        for hb in range(2):
                            s_bc = sin[:, :, hb, :].unsqueeze(1).to_broadcast([P, nh, 2, 16])
                            dve.tensor_tensor(turned_h[:, :, :, hb, :], halves[:, :, :, 1 - hb, :], s_bc, ALU.mult).then_inc(s_r, 1)
                        dve.tensor_tensor(outs[0], heads, cos, ALU.mult).then_inc(s_r, 1)
                        n_rope[0] += 3
                        dve.wait_ge(s_r, n_rope[0])
                        tv = z_t[:, 0:w].rearrange("p (h d) -> p h d", d=HD)
                        if c == CH_KVG:
                            step(dve.tensor_tensor(outs[0], outs[0], tv, ALU.add))
                            dve.tensor_copy(outs[1], outs[0]).then_inc(s_rope, 1)
                        else:
                            dve.tensor_tensor(outs[0], outs[0], tv, ALU.add).then_inc(s_rope, 1)

                    def maxima(i):
                        for n in range(first_map[i], map_end[i]):
                            t = maps[n][2]
                            dve.wait_ge(t_s, n + 1)
                            if n >= 4:
                                dve.wait_ge(t_p, max(j for j in range(len(att)) if first_map[j] <= n - 4) + 1)
                            dve.tensor_reduce(small[:, n % 4, 0:1], scores_view(n, t), AX.X if t == 0 else AX.XY,
                                              ALU.max, negate=True).then_inc(t_max, 1)

                    n_inv = [0]

                    def normalise(i):
                        kind, h, t = att[i]
                        n = first_map[i]
                        w = P if t == 0 else KEYS
                        dve.wait_ge(t_exp, map_end[i])
                        for j in range(n, map_end[i]):
                            dve.reciprocal(small[:, j % 4, 2:3], small[:, j % 4, 1:2]).then_inc(t_l, 1)
                            n_inv[0] += 1
                        dve.wait_ge(t_l, n_inv[0])
                        p0 = prob[:, n % 4, 0:w]
                        if kind == "g":
                            dve.tensor_scalar(p0, p0, small[:, n % 4, 2:3], None, ALU.mult).then_inc(t_p, 1)
                            return
                        p1 = prob[:, (n + 1) % 4, 0:w]
                        dve.tensor_scalar(p0, p0, small[:, n % 4, 2:3], None, ALU.mult).then_inc(t_l, 1)
                        dve.tensor_scalar(small[:, n % 4, 3:4], small[:, (n + 1) % 4, 2:3], neg_lam[:, 0:1], None,
                                          ALU.mult).then_inc(t_l, 1)
                        n_inv[0] += 2
                        dve.wait_ge(t_l, n_inv[0])
                        dve.scalar_tensor_tensor(out=p0, in0=p1, scalar=small[:, n % 4, 3:4], in1=p0,
                                                 op0=ALU.mult, op1=ALU.add).then_inc(t_p, 1)

                    def keep_o(i):
                        kind, h, t = att[i]
                        bank = psum[:, 6 + i % 2, 0:P]
                        if att[i] == ("d", 0, 0):
                            dve.wait_ge(s_store, 16 * 4)
                        dve.wait_ge(t_pv, i + 1)
                        if kind == "g":
                            r = HD * (h % 2)
                            dve.tensor_copy(q_T[r:r + HD, h // 2, t * P:(t + 1) * P], bank[r:r + HD, :]).then_inc(t_o, 1)
                        else:
                            dve.tensor_copy(od[:, t, h, :], bank).then_inc(t_o, 1)

                    for i in range(len(att) + 3):
                        if i < len(att):
                            maxima(i)
                        if 1 <= i < len(att) + 1:
                            normalise(i - 1)
                        if i >= 3:
                            keep_o(i - 3)
                    dve.wait_ge(m2_tr, MC2)
                    dve.wait_ge(t_pt, len(att))
                    rest = mod_T[:, MB2:48, :]
                    dve.tensor_tensor(rest, psum[:, 5, P:P + 2 * (48 - MB2)].rearrange("p (c s) -> p c s", s=2), rest,
                                      ALU.add).then_inc(m2_cp, 1)
                    dve.wait_ge(m2_cp, 1)
                    scaled_gain(mul2, 32, 8).then_inc(m2_cp, 1)
                    dve.wait_ge(d_sq, TT * DH)
                    dve.tensor_scalar(od_ss[:, :], od_ss[:, :], 1.0 / (2 * HD), EPS, ALU.mult, ALU.add).then_inc(d_1, 1)
                    dve.wait_ge(d_2, 1)
                    dve.reciprocal(od_ss[:, :], od_r[:, :]).then_inc(d_1, 1)
                    dve.wait_ge(d_1, 2)
                    for h in range(DH):
                        rs = od_ss[:, :].rearrange("p (t h) -> p t h", h=DH)[:, :, h]
                        dve.tensor_tensor(od[:, :, h, :], od[:, :, h, :], rs.unsqueeze(2).to_broadcast([P, TT, P]),
                                          ALU.mult).then_inc(d_3, 1)
                    n_acc = 0
                    for m in range(4):
                        for b in range(3):
                            for fc in range(2):
                                g = 6 * m + 2 * b + fc
                                if g == 0:
                                    dve.wait_ge(d_t, DH)
                                dve.wait_ge(g_sig, g + 1)
                                dve.wait_ge(g_pfull, g + 1)
                                src = pair(2 + g % 2)[:, :, 0:HALF]
                                sg = sig_m[:, g % 2, :].rearrange("p (a b) -> p a b", a=2)
                                if b == 0:
                                    if m >= 1:
                                        dve.wait_ge(g_lo, 2 * m)
                                    dst = mg[:, fc, :]
                                else:
                                    dst = mg_t[:, :]
                                dve.tensor_tensor(dst.rearrange("p (a b) -> p a b", a=2), src, sg, ALU.mult).then_inc(g_pfree, 1)
                                if b > 0:
                                    dve.wait_ge(g_pfree, g + 1)
                                    dve.tensor_tensor(mg[:, fc, :], mg[:, fc, :], mg_t[:, :], ALU.add).then_inc(g_acc, 1)
                                    n_acc += 1
                                    dve.wait_ge(g_acc, n_acc)
                    for f in range(KD):
                        dve.wait_ge(o_full, f + 1)
                        add_gated(dve, f, pair(f % 3), gate1, o_add)
                    rstd_of(dve, n2, var2, rstd2)

                @block.tensor
                def _(pe):
                    for kc in range(KD):
                        sum_squares(pe, n1, sq_mix, kc)
                    pe.wait_ge(s_small, 16 * 8)
                    pe.transpose(psum[:, 4, 0:64], row_in[:, :], ident[0:64, 0:64])

                    def turn_mod(j):
                        pe.wait_ge(m_ev, 4 * (j + 1))
                        for q in range(4):
                            c = 4 * j + q
                            mm = pe.matmul(psum[:, 5, 2 * c:2 * c + 2], mod_rows[:, j % 2, q * P:(q + 1) * P],
                                           row_sum[:, :], start=True, stop=True)
                        mm.then_inc(m_tr, 1)

                    for j in range(MC):
                        pe.wait_ge(m_ld[j % 3], 16 * (j // 3 + 1))
                        if j >= 2:
                            pe.wait_ge(m_ev, 4 * (j - 1))
                        for kc in range(KD):
                            q = kc % 4
                            mm = pe.matmul(psum[32 * q:32 * q + 2, j % 2, :], cond_T[:, kc, :], wm[j % 3][:, kc, :],
                                           start=(kc < 4), stop=(kc >= 4))
                        mm.then_inc(m_mm, 1)
                        if j >= 1:
                            turn_mod(j - 1)
                    turn_mod(MC - 1)
                    pe.wait_ge(m_done, 1)

                    def feature_major(dst, i, fc, mv_hi, mv_lo, waits=None):
                        for kc in range(KD):
                            if waits is not None:
                                pe.wait_ge(waits, kc + 1)
                            cs = slice(fc * P, (fc + 1) * P)
                            mm = mm_split(pe, [dst[:, 0, 0:HALF], dst[:, 1, 0:HALF]],
                                          whi[i % 2][:, kc, cs], wlo[i % 2][:, kc, cs],
                                          [mv_hi[:, kc, 0:HALF], mv_hi[:, kc, HALF:TOK]],
                                          [mv_lo[:, kc, 0:HALF], mv_lo[:, kc, HALF:TOK]], kc == 0, kc == KD - 1)
                        return mm

                    for n, u in enumerate(units):
                        if n >= 4:
                            pe.wait_ge(s_free, n - 3)
                        if u[0] == "u":
                            g = u[1]
                            pe.wait_ge(w_lo, g // 2 + 1)
                            mm = feature_major(pair(n), g // 2, g % 2, h_hi, h_lo, n_lo if g == 0 else None)
                            mm.then_inc(s_full, 1)
                        elif u[0] == "ab":
                            g, part = u[1:]
                            if (g, part) == (0, 0):
                                pe.wait_ge(s_small, 16 * 12)
                            pe.wait_ge(s_free, unit_no[("u", g)] + 1)
                            for t in ((0, 1, 2, 3), (4,))[part]:
                                mm = pe.matmul(flat(n)[:, (t % 4) * 2 * P:(t % 4 + 1) * 2 * P], u_T[:, g, t * P:(t + 1) * P],
                                               dft_ch[:, :], start=True, stop=True)
                            mm.then_inc(s_full, 1)
                        elif u[0] == "y":
                            g = u[1]
                            pe.wait_ge(s_free, unit_no[("ab", g, 1)] + 1)
                            for part in range(2):
                                pe.matmul(pair(n)[:, 0, 0:P], ab[:, g % 2, 0, part * P:(part + 1) * P], dft_pr[:, part, :],
                                          start=(part == 0), stop=(part == 1))
                            for t in range(4):
                                for part in range(2):
                                    mm = pe.matmul(pair(n)[:, 1, :], ab[:, g % 2, t + 1, part * P:(part + 1) * P],
                                                   dft_tab[:, part, t, :], start=(t == 0 and part == 0),
                                                   stop=(t == 3 and part == 1))
                            mm.then_inc(s_full, 1)
                        elif u[0] == "kcache":
                            pe.wait_ge(s_kc, 48)
                            for c in range(6):
                                mm = pe.transpose(flat(n)[:, c * P:(c + 1) * P], k_cache[:, c, :], ident[:, :])
                            mm.then_inc(s_full, 1)
                        elif u[0] == "z":
                            c, t = u[1:]
                            pe.wait_ge(w_lo, c + 1)
                            ts = slice(t * P, (t + 1) * P)
                            for kc in range(KD):
                                mm = mm_split(pe, [flat(n)[:, 0:WC]], h_hi[:, kc, ts], h_lo[:, kc, ts],
                                              [whi[c % 2][:, kc, :]], [wlo[c % 2][:, kc, :]], kc == 0, kc == KD - 1)
                            mm.then_inc(s_full, 1)
                        else:
                            c, t = u[1:]
                            i = n_x[(c, t)]
                            pe.wait_ge(s_rope, i + 1)
                            for q in range(2):
                                mm = pe.transpose(flat(n)[:, q * P:(q + 1) * P], z_r[:, i % 4, q * P:(q + 1) * P], ident[:, :])
                            mm.then_inc(s_full, 1)

                    def scores(i):
                        for n in range(first_map[i], map_end[i]):
                            kind, h, t, m = maps[n]
                            pe.wait_ge(t_q, n + 1)
                            if n >= 2:
                                pe.wait_ge(t_exp, n - 1)
                            if t == 0:
                                mm = pe.matmul(flat(n % 2)[:, 0:P], q_pad[:, n % 4, :], k_slice(kind, h, 5 * P, 6 * P),
                                               start=True, stop=True)
                            else:
                                for hf in range(2):
                                    mm = pe.matmul(pair(n % 2)[:, hf, 0:HALF], q_pad[:, n % 4, :],
                                                   k_slice(kind, h, hf * HALF, (hf + 1) * HALF), start=True, stop=True)
                            mm.then_inc(t_s, 1)

                    def mod_rest(k):
                        pe.wait_ge(m2_ld[k % 2], 16 * (k // 2 + 1))
                        for kc in range(KD):
                            q = kc % 4
                            mm = pe.matmul(psum[32 * q:32 * q + 2, 5, 256:512], cond_T[:, kc, :],
                                           raw[(N_WIN + k) % 2][:, kc, :], start=(kc < 4), stop=(kc >= 4))
                        mm.then_inc(m2_mm, 1)

                    def turn_mod_rest(k):
                        for q in range(2):
                            c = P + 2 * (2 * k + q)
                            mm = pe.matmul(psum[:, 5, c:c + 2], mod_rows2[:, k % 2, q * P:(q + 1) * P], row_sum[:, :],
                                           start=True, stop=True)
                        mm.then_inc(m2_tr, 1)

                    def turn(i):
                        if i >= 1:
                            pe.wait_ge(t_pt, i)
                            if mod_step(i - 1) is not None:
                                pe.wait_ge(m2_ev, 4 * (mod_step(i - 1) + 1))
                        k = mod_step(i)
                        if k is not None:
                            if k >= 1:
                                turn_mod_rest(k - 1)
                            mod_rest(k)
                        if i == MOD_END:
                            turn_mod_rest(MC2 - 1)
                        pe.wait_ge(t_p, i + 1)
                        for j in range(len(key_tiles(att[i][2]))):
                            mm = pe.transpose(flat(2)[:, j * P:(j + 1) * P], prob[:, first_map[i] % 4, j * P:(j + 1) * P],
                                              ident[:, :])
                        mm.then_inc(t_tr, 1)

                    def values(i):
                        kind, h, t = att[i]
                        tiles = key_tiles(t)
                        pe.wait_ge(t_pt, i + 1)
                        if i == 0:
                            pe.wait_ge(s_cv, 32)
                        if i >= 2:
                            pe.wait_ge(t_o, i - 1)
                        for j, kt in enumerate(tiles):
                            st, sp_ = j == 0, j == len(tiles) - 1
                            if kind == "g":
                                r = HD * (h % 2)
                                v0 = HD * (h // (QH // KVH))
                                mm = pe.matmul(psum[r:r + HD, 6 + i % 2, 0:P], v_tok[:, kt, v0:v0 + HD],
                                               prob_T[:, i % 2, j, :], start=st, stop=sp_)
                            else:
                                mm = pe.matmul(psum[:, 6 + i % 2, 0:P], prob_T[:, i % 2, j, :],
                                               v_tok[:, kt, P + h * P:P + (h + 1) * P], start=st, stop=sp_)
                        mm.then_inc(t_pv, 1)

                    pe.wait_ge(s_free, len(units))
                    for i in range(len(att) + 3):
                        if i < len(att):
                            scores(i)
                        if 2 <= i < len(att) + 2:
                            turn(i - 2)
                        if i >= 3:
                            values(i - 3)
                    def turn_diff():
                        for h in range(DH):
                            pe.wait_ge(d_3, h + 1)
                            if h < 2:
                                pe.wait_ge(g_sig, h + 1)
                            else:
                                pe.wait_ge(d_k, h - 1)
                            for t in range(TT):
                                mm = pe.transpose(flat(h % 2)[:, t * P:(t + 1) * P], od[:, t, h, :], ident[:, :])
                            mm.then_inc(d_t, 1)
                        pe.wait_ge(d_k, DH)

                    pe.wait_ge(t_exp, len(maps))
                    pe.wait_ge(t_pt, len(att))
                    pe.wait_ge(m2_cp, 1)
                    pe.wait_ge(t_o, len(att))
                    branch = (y_T, q_T[:, 0:4, :], q_T[:, 4:8, :])
                    for m in range(4):
                        for b in range(3):
                            i = N_WIN + 3 * m + b
                            n_p = 3 * m + b
                            pe.wait_ge(w_lo, i + 1)
                            for fc in range(2):
                                g = 6 * m + 2 * b + fc
                                if g >= 2:
                                    pe.wait_ge(g_sig, g - 1)
                                mm = feature_major(pair(g % 2), i, fc, h_hi, h_lo)
                                mm.then_inc(g_full, 1)
                                pe.wait_ge(p_ld[n_p % 2], 16 * (n_p // 2 + 1))
                                if g >= 2:
                                    pe.wait_ge(g_pfree, g - 1)
                                for kc in range(4):
                                    for hf in range(2):
                                        mm = pe.matmul(pair(2 + g % 2)[:, hf, 0:HALF], pw[n_p % 2][:, kc, fc * P:(fc + 1) * P],
                                                       branch[b][:, kc, hf * HALF:(hf + 1) * HALF],
                                                       start=(kc == 0), stop=(kc == 3))
                                mm.then_inc(g_pfull, 1)
                            if n_p == 0:
                                turn_diff()
                    pe.wait_ge(g_sig, 23)
                    for f in range(KD):
                        i = N_WIN + 12 + f // 2
                        pe.wait_ge(w_lo, i + 1)
                        if f == 1:
                            pe.wait_ge(g_sig, 24)
                            pe.wait_ge(g_pfree, 24)
                        if f >= 3:
                            pe.wait_ge(o_add, f - 2)
                        feature_major(pair(f % 3), i, f % 2, mg_hi, mg_lo, g_lo if f == 0 else None).then_inc(o_full, 1)
                        if f >= 1:
                            sum_squares(pe, n2, sq2, f - 1)
                    sum_squares(pe, n2, sq2, KD - 1)
            clear()

            with nc.Block() as block:
                @block.sync
                def _(sp):
                    src = {"g": a["w_e_gate"][layer], "u": a["w_e_up"][layer], "d": a["w_e_down"][layer]}

                    def load(r, e):
                        w = src[r][e].rearrange("(k p) n -> p k n", p=P)
                        sp.dma_start(ex[r][0][:, :, :], w).then_inc(x_ld[r], 16)

                    def load_combine(e):
                        sp.dma_start(cb[:, 0, :], comb_dram[e].partition_broadcast(P)).then_inc(c_ld, 16)

                    load("g", 0)
                    load("u", 0)
                    load("d", 0)
                    for r in "gu":
                        sp.wait_ge(x_lo[r], 1)
                        load(r, 1)
                    sp.wait_ge(r_ce, 1)
                    sp.dma_start(comb_dram, comb_T[:, :]).then_inc(r_cs, 16)
                    sp.wait_ge(r_cs, 16)
                    load_combine(0)
                    sp.wait_ge(x_sg, 2)
                    load_combine(1)
                    sp.wait_ge(x_lo["d"], 1)
                    load("d", 1)
                    with sp.Fori(2, NE) as e:
                        for r in "gud":
                            sp.wait_ge(x_lo[r], e)
                            load(r, e)
                            if r == "u":
                                sp.wait_ge(x_sg, 2 * e)
                                load_combine(e)

                @block.gpsimd
                def _(pool):
                    def lo(r, e):
                        pool.wait_ge(x_hi[r], e + 1)
                        pool.tensor_tensor(ex[r][2][:, :, :], ex[r][0][:, :, :], ex[r][1][:, :, :].bitcast(F32),
                                           ALU.subtract).then_inc(x_lo[r], 1)

                    def act_low(e):
                        pool.wait_ge(x_ahi, e + 1)
                        pool.tensor_tensor(act_lo[:, :, :], act_f[:, :, :], act_hi[:, :, :].bitcast(F32),
                                           ALU.subtract).then_inc(x_alo, 1)
                    for kc in range(KD):
                        if kc == NH:
                            lo("g", 0)
                        modulate_pool(pool, h_moe, kc)
                    lo("u", 0)
                    pool.memset(y_acc[:, :, :], 0.0).then_inc(x_y0, 1)
                    lo("g", 1)
                    lo("u", 1)

                    def body(e, last=False):
                        act_low(e - 1)
                        lo("d", e - 1)
                        if not last:
                            lo("g", e + 1)
                            lo("u", e + 1)
                    with pool.Fori(1, NE - 1) as e:
                        body(e)
                    body(NE - 1, last=True)
                    act_low(NE - 1)
                    lo("d", NE - 1)

                @block.scalar
                def _(act):
                    def hi(r, e, used=None):
                        act.wait_ge(x_ld[r], 16 * (e + 1))
                        if used is not None:
                            act.wait_ge(x_full, used)
                        act.activation(ex[r][1][:, :, :], ex[r][0][:, :, :], ACT.Copy).then_inc(x_hi[r], 1)

                    def sigmoid(e, fc):
                        act.wait_ge(x_full, 12 * e - 8 + fc + 1)
                        act.activation(sig_x[:, fc, :].rearrange("p (a b) -> p a b", a=2), pair(fc)[:, :, 0:HALF],
                                       ACT.Sigmoid).then_inc(x_sig, 1)

                    def act_high(e, kept, used=None):
                        act.wait_ge(x_free, kept)
                        if used is not None:
                            act.wait_ge(x_full, used)
                        act.activation(act_hi[:, :, :], act_f[:, :, :], ACT.Copy).then_inc(x_ahi, 1)

                    for kc in range(KD):
                        if kc == NH:
                            hi("g", 0)
                        modulate_act(act, h_moe, mul2, shift2, kc)
                        if kc == 5:
                            hi("u", 0)
                    act.wait_ge(r_lg, 1)
                    act.activation(logits[:, :].rearrange("p (a b) -> p a b", a=2), pair(3)[0:NE, :, 0:HALF],
                                   ACT.Copy).then_inc(r_lk, 1)
                    act.wait_ge(r_lt, 1)
                    act.activation(sc[:, :], psum[:, 4, 0:TT * NE], ACT.Sigmoid).then_inc(r_sg, 1)
                    for fc in range(2):
                        act.wait_ge(x_full, fc + 1)
                        act.activation(sig_x[:, fc, :].rearrange("p (a b) -> p a b", a=2), pair(fc)[:, :, 0:HALF],
                                       ACT.Sigmoid).then_inc(x_sig, 1)
                    hi("g", 1, 2)
                    act.wait_ge(r_ct, 1)
                    act.activation(comb_T[:, :], flat(0)[0:NE, 0:TOK], ACT.Copy).then_inc(r_ce, 1)
                    hi("u", 1, 4)

                    def body(e, last=False):
                        u0 = 12 * e - 8
                        one = isinstance(e, int) and e == 1
                        act_high(e - 1, 4 if one else u0 - 8, None if one else u0)
                        hi("d", e - 1, None if one else u0)
                        for fc in range(2):
                            sigmoid(e, fc)
                        if not last:
                            hi("g", e + 1, u0 + 2)
                            hi("u", e + 1, u0 + 4)
                    body(1)
                    with act.Fori(2, NE - 1) as e:
                        body(e)
                    body(NE - 1, last=True)
                    act_high(NE - 1, 12 * NE - 16, 12 * NE - 8)
                    hi("d", NE - 1, 12 * NE - 8)

                @block.vector
                def _(dve):
                    modulate_dve(dve, h_moe, rstd2)
                    n_st = [0]

                    def step(ins):
                        n_st[0] += 1
                        ins.then_inc(r_st, 1)
                        dve.wait_ge(r_st, n_st[0])

                    def ranks(dst, v, n):
                        jj = v.unsqueeze(3).to_broadcast([P, n, 4, 4])
                        ii = v.unsqueeze(2).to_broadcast([P, n, 4, 4])
                        gt = cmp_gt[:, 0:n * 16].rearrange("p (n j i) -> p n j i", j=4, i=4)
                        eq = cmp_eq[:, 0:n * 16].rearrange("p (n j i) -> p n j i", j=4, i=4)
                        step(dve.tensor_tensor(gt, ii, jj, ALU.is_gt))
                        step(dve.tensor_tensor(eq, ii, jj, ALU.is_equal))
                        step(dve.tensor_tensor(eq.rearrange("p n j i -> p n (j i)"), eq.rearrange("p n j i -> p n (j i)"),
                                               tie[:, :, :].rearrange("p j i -> p (j i)").unsqueeze(1).to_broadcast([P, n, 16]),
                                               ALU.mult))
                        step(dve.tensor_tensor(cmp_gt[:, 0:n * 16], cmp_gt[:, 0:n * 16], cmp_eq[:, 0:n * 16], ALU.add))
                        step(dve.tensor_reduce(dst, gt.rearrange("p n j i -> p (n j) i"), AX.X, ALU.add))

                    dve.wait_ge(r_sg, 1)
                    e3 = lambda x: x[:, :].rearrange("p (t e) -> p t e", e=NE)
                    step(dve.tensor_tensor(e3(sel), e3(sc), bias_bc[:, :].unsqueeze(1).to_broadcast([P, TT, NE]), ALU.add))
                    ranks(rank[:, :], sel[:, :].rearrange("p (n j) -> p n j", j=4), TT * NG)
                    step(dve.tensor_scalar(top2[:, :], rank[:, :], 1.5, None, ALU.is_lt))
                    step(dve.tensor_tensor(tmp16[:, :], top2[:, :], sel[:, :], ALU.mult))
                    step(dve.tensor_reduce(grp[:, :], tmp16[:, :].rearrange("p (n j) -> p n j", j=4), AX.X, ALU.add))
                    ranks(grank[:, :], grp[:, :].rearrange("p (n j) -> p n j", j=4), TT)
                    step(dve.tensor_scalar(gbest[:, :], grank[:, :], 0.5, None, ALU.is_lt))
                    g3 = lambda x: x[:, :].rearrange("p (n j) -> p n j", j=4)
                    step(dve.tensor_tensor(g3(top2), g3(top2), gbest[:, :].unsqueeze(2).to_broadcast([P, TT * NG, 4]), ALU.mult))
                    step(dve.tensor_tensor(tmp16[:, :], top2[:, :], sc[:, :], ALU.mult))
                    step(dve.tensor_reduce(wsum[:, :], e3(tmp16), AX.X, ALU.add))
                    step(dve.reciprocal(wrec[:, :], wsum[:, :]))
                    step(dve.tensor_tensor(e3(comb), e3(tmp16), wrec[:, :].unsqueeze(2).to_broadcast([P, TT, NE]), ALU.mult))
                    dve.wait_ge(x_y0, 1)

                    def halves(v):
                        return v.rearrange("p (a b) -> p a b", a=2)

                    def gated(e, fc):
                        dve.wait_ge(x_sig, 2 * e + fc + 1)
                        dve.tensor_tensor(halves(sig_x[:, fc, :]), pair(fc)[:, :, 0:HALF], halves(sig_x[:, fc, :]),
                                          ALU.mult).then_inc(x_free, 1)

                    def combined(e, fc, free):
                        dve.wait_ge(c_ld, 16 * (e + 1))
                        dve.wait_ge(x_free, free)
                        ins = dve.tensor_tensor(sig_x[:, fc, :], sig_x[:, fc, :], cb[:, 0, :], ALU.mult).then_inc(x_sg, 1)
                        return ins

                    def activated(e, fc, full):
                        dve.wait_ge(x_full, full)
                        dve.wait_ge(x_sg, 2 * e + fc + 1)
                        dve.tensor_tensor(halves(act_f[:, fc, :]), pair(2 + fc)[:, :, 0:HALF], halves(sig_x[:, fc, :]),
                                          ALU.mult).then_inc(x_free, 1)

                    def down(u0):
                        for f in range(KD):
                            dve.wait_ge(x_full, u0 + f + 1)
                            dve.tensor_tensor(halves(y_acc[:, f, :]), pair(f)[:, :, 0:HALF], halves(y_acc[:, f, :]),
                                              ALU.add).then_inc(x_free, 1)

                    def expert(e, u0, up=(3, 4)):
                        gated(e, 0)
                        gated(e, 1)
                        combined(e, 0, u0 + 1)
                        combined(e, 1, u0 + 2)
                        activated(e, 0, u0 + up[0])
                        activated(e, 1, u0 + up[1])

                    expert(0, 0, (4, 4))
                    with dve.Fori(1, NE) as e:
                        dve.wait_ge(x_alo, e)
                        expert(e, 12 * e - 8)
                        down(12 * e - 4)
                    down(12 * NE - 8)
                    dve.wait_ge(x_free, 12 * NE)
                    for f in range(KD):
                        for s, (c0, c1) in enumerate(((0, N_PROMPT), (N_PROMPT, TOK))):
                            dve.scalar_tensor_tensor(out=x_T[:, f, c0:c1], in0=y_acc[:, f, c0:c1], scalar=gate2[:, f, s:s + 1],
                                                     in1=x_T[:, f, c0:c1], op0=ALU.mult, op1=ALU.add).then_inc(x_step, 1)

                @block.tensor
                def _(pe):
                    def up_or_gate(r, fc, slot, free=None, chunks=None, beside=None):
                        if free is not None:
                            pe.wait_ge(x_free, free)
                        cs = slice(fc * P, (fc + 1) * P)
                        dst = pair(slot)
                        for kc in range(KD):
                            if chunks is not None:
                                pe.wait_ge(chunks, kc + 1)
                            if beside is not None:
                                beside(kc)
                            mm = mm_split(pe, [dst[:, 0, 0:HALF], dst[:, 1, 0:HALF]], ex[r][1][:, kc, cs], ex[r][2][:, kc, cs],
                                          [h_hi[:, kc, 0:HALF], h_hi[:, kc, HALF:TOK]],
                                          [h_lo[:, kc, 0:HALF], h_lo[:, kc, HALF:TOK]], kc == 0, kc == KD - 1)
                        mm.then_inc(x_full, 1)

                    def down(e, u0):
                        pe.wait_ge(x_lo["d"], e + 1)
                        pe.wait_ge(x_alo, e + 1)
                        for f in range(KD):
                            pe.wait_ge(x_free, u0 + f - 3)
                            cs = slice(f * P, (f + 1) * P)
                            dst = pair(f)
                            for kc in range(2):
                                mm = mm_split(pe, [dst[:, 0, 0:HALF], dst[:, 1, 0:HALF]],
                                              ex["d"][1][:, kc, cs], ex["d"][2][:, kc, cs],
                                              [act_hi[:, kc, 0:HALF], act_hi[:, kc, HALF:TOK]],
                                              [act_lo[:, kc, 0:HALF], act_lo[:, kc, HALF:TOK]], kc == 0, kc == 1)
                            mm.then_inc(x_full, 1)

                    pe.wait_ge(x_lo["g"], 1)

                    def router(kc):
                        for n, (hp, wp) in enumerate(((h_hi, wr_hi), (h_hi, wr_lo), (h_lo, wr_hi), (h_lo, wr_lo))):
                            for hf in range(2):
                                mm = pe.matmul(pair(3)[0:NE, hf, 0:HALF], wp[:, kc, :], hp[:, kc, hf * HALF:(hf + 1) * HALF],
                                               start=(kc == 0 and n == 0), stop=(kc == KD - 1 and n == 3))
                        if kc == KD - 1:
                            mm.then_inc(r_lg, 1)

                    up_or_gate("g", 0, 0, chunks=n_lo, beside=router)
                    pe.wait_ge(r_lk, 1)
                    for t in range(TT):
                        mm = pe.transpose(psum[:, 4, t * NE:(t + 1) * NE], logits[:, t * P:(t + 1) * P], ident[0:NE, 0:NE])
                    mm.then_inc(r_lt, 1)
                    up_or_gate("g", 1, 1)
                    pe.wait_ge(x_lo["u"], 1)
                    up_or_gate("u", 1, 3)
                    pe.wait_ge(r_sg, 1)
                    up_or_gate("u", 0, 2)
                    pe.wait_ge(r_st, ROUTE_STEPS)
                    pe.wait_ge(x_free, 1)
                    for t in range(TT):
                        mm = pe.transpose(flat(0)[0:NE, t * P:(t + 1) * P], comb[:, t * NE:(t + 1) * NE], ident[:, :])
                    mm.then_inc(r_ct, 1)
                    pe.wait_ge(r_ce, 1)
                    with pe.Fori(1, NE) as e:
                        u0 = 12 * e - 8
                        for n, r in enumerate("gu"):
                            pe.wait_ge(x_lo[r], e + 1)
                            for fc in range(2):
                                up_or_gate(r, fc, 2 * n + fc, u0 + 2 * n + fc - 3)
                        down(e - 1, u0 + 4)
                    down(NE - 1, 12 * NE - 8)
            clear()

        y_tok = at("y_tok", [P, 2, D], Z)
        sq_fin = at("sq_fin", [P, 2, TOK], Z + 20 * K)
        var_fin = at("var_fin", [P, TOK], Z + 25 * K)
        rstd_fin = at("rstd_fin", [P, TOK], Z + 28 * K)
        h_raw = at("h_raw", [P, 2, TOK], Z + 31 * K)
        h_fin = at("h_final", [P, KD, TOK], Z + 40 * K)
        f_t, f_e = sem("out_turned"), sem("out_kept")
        f_s = [sem(f"out_stored{i}") for i in range(2)]
        with nc.Block() as block:
            @block.scalar
            def _(act):
                for kc in range(KD):
                    square(act, nf, sq_fin, kc)
                root(act, nf, var_fin)
                for kc in range(KD):
                    act.wait_ge(n_t, kc + 1)
                    act.activation(h_fin[:, kc, :], h_raw[:, kc % 2, :], ACT.Copy,
                                   scale=fin_gain[:, kc:kc + 1]).then_inc(n_h, 1)

            @block.vector
            def _(dve):
                rstd_of(dve, nf, var_fin, rstd_fin)
                dve.wait_ge(nf[4], 1)
                for kc in range(KD):
                    if kc >= 2:
                        dve.wait_ge(n_h, kc - 1)
                    dve.tensor_tensor(h_raw[:, kc % 2, :], x_T[:, kc, :], rstd_fin[:, :], ALU.mult).then_inc(n_t, 1)
                for t in range(TT):
                    dve.wait_ge(f_t, t + 1)
                    if t >= 2:
                        dve.wait_ge(f_s[t % 2], 16 * (t // 2))
                    dve.tensor_copy(y_tok[:, t % 2, :], flat(t % 3)[:, :]).then_inc(f_e, 1)

            @block.tensor
            def _(pe):
                for kc in range(KD):
                    sum_squares(pe, nf, sq_fin, kc)
                pe.wait_ge(n_h, KD)
                for t in range(TT):
                    if t >= 3:
                        pe.wait_ge(f_e, t - 2)
                    for kc in range(KD):
                        mm = pe.transpose(flat(t % 3)[:, kc * P:(kc + 1) * P], h_fin[:, kc, t * P:(t + 1) * P], ident[:, :])
                    mm.then_inc(f_t, 1)

            @block.sync
            def _(sp):
                for t in range(TT):
                    sp.wait_ge(f_e, t + 1)
                    dst = a["y_prompt"][0] if t == 0 else a["y_sample"][0, (t - 1) * P:t * P, :]
                    sp.dma_start(dst, y_tok[:, t % 2, :]).then_inc(f_s[t % 2], 16)
                sp.wait_ge(f_s[0], 16 * ((TT + 1) // 2))
                sp.wait_ge(f_s[1], 16 * (TT // 2))


def constants():
    f = np.float32
    c = {"c_ident": np.eye(P, dtype=f), "c_ones": np.ones((P, P), f)}
    j = np.arange(4)
    c["c_row_sum"] = np.array([[float(p % 32 == s) for s in range(2)] for p in range(P)], f)
    c["c_tie"] = (j[None, :] < j[:, None]).astype(f)
    init = [0.8 - 0.6 * np.exp(-0.3 * l) for l in range(DEPTH)]
    c["c_lambda"] = np.array([[x, 1.0 - x] for x in init], f)

    def dft(n):
        k = np.arange(n)
        ang = 2 * np.pi * ((k[:, None] * k[None, :]) % n) / n
        return np.cos(ang), -np.sin(ang)
    ch_c, ch_s = dft(FGD)
    c["c_dft_ch"] = np.concatenate([ch_c, ch_s], 1).astype(f)
    sc_, ss_ = dft(N_SAMPLE)
    nrm = 1.0 / np.sqrt(N_SAMPLE * FGD)
    tab = np.stack([sc_ * nrm, -ss_ * nrm])
    c["c_dft"] = np.ascontiguousarray(tab.reshape(2, 4, P, N_SAMPLE).transpose(2, 0, 1, 3)).astype(f)
    pc_, ps_ = dft(N_PROMPT)
    nrm = 1.0 / np.sqrt(N_PROMPT * FGD)
    c["c_dft_pr"] = np.ascontiguousarray(np.stack([pc_ * nrm, -ps_ * nrm], 1)).astype(f)
    grid_w, axis = 64, HD // 2
    pos = np.arange(N_SAMPLE)
    inv = (f(10000.0) ** (-(np.arange(axis // 2, dtype=f) * f(2.0) / f(axis)))).astype(f)
    ar = ((pos // grid_w).astype(f)[:, None] * inv[None, :]).astype(f)
    ac = ((pos % grid_w).astype(f)[:, None] * inv[None, :]).astype(f)
    ang = np.concatenate([ar, ar, ac, ac], -1)
    sign = np.repeat(np.array([-1, 1, -1, 1], f), 16)
    rp = np.stack([np.cos(ang), np.sin(ang) * sign])
    c["c_rope"] = np.ascontiguousarray(rp.reshape(2, 4, P, HD).transpose(2, 0, 1, 3)).astype(f)
    return c


INS = ["x_prompt", "x_sample", "cache_gqa_k", "cache_gqa_v", "cache_diff_k", "cache_diff_v", "c", "c_ctx",
       "norm1_g", "w_mod", "b_mod", "w_in", "gqa_q_norm", "gqa_k_norm", "diff_lambda", "diff_subln_g",
       "w_fourier", "w_gqa_o", "w_diff_o", "w_out", "norm2_g", "w_router", "router_bias", "w_e_gate",
       "w_e_up", "w_e_down", "final_norm_g"]
OUTS = [("y_prompt", (1, N_PROMPT, D)), ("y_sample", (1, N_SAMPLE, D)),
        ("new_gqa_k", (1, DEPTH, N_PROMPT, KVH, HD)), ("new_gqa_v", (1, DEPTH, N_PROMPT, KVH, HD)),
        ("new_diff_k", (1, DEPTH, N_PROMPT, DH, 2, HD)), ("new_diff_v", (1, DEPTH, N_PROMPT, DH, 2 * HD))]


def kernel(**inputs):
    import concourse.bacc as bacc
    from concourse.bass_utils import run_bass_kernel_spmd

    nc = bacc.Bacc("TRN2", target_bir_lowering=False, num_devices=1)
    arrays = {n: np.ascontiguousarray(inputs[n]) for n in INS}
    arrays.update(constants())
    aps = {n: nc.dram_tensor(n, v.shape, F32, kind="ExternalInput").ap() for n, v in arrays.items()}
    for n, shape in OUTS:
        aps[n] = nc.dram_tensor(n, shape, F32, kind="ExternalOutput").ap()
    build(nc, aps)
    r = run_bass_kernel_spmd(nc, [arrays], core_ids=[0])
    return tuple(r.results[0][n] for n, _ in OUTS)
```
